# Optimizing a Trainium2 kernel written in Bass

```python
import math
import numpy as np
import jax
import jax.numpy as jnp
from jax import lax
import jax, jax.numpy as jnp

D_MODEL = 1024
BATCH = 1
SEQ = 512
DEPTH = 2

GRID_W = 64
CTX_LEN = 256
HEAD_DIM = 64
D_CONV = 512
CONV_K = 31
NA_HEADS = 8
NA_MAX_ROWS = 8
NA_COLS = 16
WA_HEADS = 8
WA_KV_HEADS = 2
WA_WINDOW = 128
WA_BLOCK = 128
ROPE_BASE = 10000.0
EPS = 1e-6
D_NA = NA_HEADS * HEAD_DIM
D_WA = WA_HEADS * HEAD_DIM
D_WA_KV = WA_KV_HEADS * HEAD_DIM
SPLIT_SIZES = (2 * D_CONV, D_CONV, D_NA, D_NA, D_NA, D_NA, D_WA, D_WA_KV, D_WA_KV, D_WA, 3 * D_MODEL)
D_IN = sum(SPLIT_SIZES)
SPLIT_POINTS = tuple(int(v) for v in np.cumsum(SPLIT_SIZES)[:-1])
SPLIT_STARTS = (0,) + SPLIT_POINTS


def rms_norm(x, g):
    xf = x.astype(jnp.float32)
    y = xf * lax.rsqrt(jnp.mean(xf * xf, axis=-1, keepdims=True) + EPS)
    return (y * g.astype(jnp.float32)).astype(x.dtype)

def layer_norm(x, g, b):
    xf = x.astype(jnp.float32)
    mu = jnp.mean(xf, axis=-1, keepdims=True)
    var = jnp.mean(jnp.square(xf - mu), axis=-1, keepdims=True)
    y = (xf - mu) * lax.rsqrt(var + EPS)
    return (y * g.astype(jnp.float32) + b.astype(jnp.float32)).astype(x.dtype)

def depthwise_conv(x, w, b):
    y = lax.conv_general_dilated(
        x, w[:, None, :].astype(x.dtype), window_strides=(1,),
        padding=[(CONV_K // 2, CONV_K // 2)],
        dimension_numbers=('NWC', 'WIO', 'NWC'),
        feature_group_count=x.shape[-1])
    return y + b

def conv_branch(u_glu, u_gate, conv_w, conv_b, ln_g, ln_b, w_proj):
    a = u_glu[..., :D_CONV] * jax.nn.sigmoid(u_glu[..., D_CONV:])
    a = depthwise_conv(a, conv_w, conv_b)
    a = jax.nn.silu(layer_norm(a, ln_g, ln_b))
    return (a * jax.nn.silu(u_gate)) @ w_proj

def split_heads(t, n):
    return t.reshape(t.shape[0], t.shape[1], n, HEAD_DIM)

def rotate(x, pos):
    half = x.shape[-1] // 2
    inv = ROPE_BASE ** (-jnp.arange(half, dtype=jnp.float32) / half)
    ang = pos.astype(jnp.float32)[:, None] * inv[None, :]
    cos = jnp.cos(ang)[None, :, None, :]
    sin = jnp.sin(ang)[None, :, None, :]
    x1 = x[..., :half].astype(jnp.float32)
    x2 = x[..., half:].astype(jnp.float32)
    return jnp.concatenate([x1 * cos - x2 * sin, x1 * sin + x2 * cos], axis=-1).astype(x.dtype)

def axial_rope(t, row_pos, col_pos):
    half = HEAD_DIM // 2
    return jnp.concatenate([rotate(t[..., :half], row_pos), rotate(t[..., half:], col_pos)], axis=-1)

def sink_softmax(s, sink):
    m = jnp.maximum(jnp.max(s, axis=-1, keepdims=True), sink)
    e = jnp.exp(s - m)
    return e / (jnp.sum(e, axis=-1, keepdims=True) + jnp.exp(sink - m))

def context_attention(q, k, v, sink):
    s = jnp.einsum('bqkgd,bnkd->bkgqn', q, k).astype(jnp.float32) * HEAD_DIM ** -0.5
    if sink is None:
        p = jax.nn.softmax(s, axis=-1)
    else:
        p = sink_softmax(s, sink.astype(jnp.float32)[None, :, :, None, None])
    o = jnp.einsum('bkgqn,bnkd->bqkgd', p.astype(v.dtype), v)
    return o.reshape(o.shape[0], o.shape[1], -1)

def neighbourhood_attention(q, k, v, k_ctx, v_ctx, rpb):
    B, S = q.shape[0], q.shape[1]
    rows = S // GRID_W
    kr = min(NA_MAX_ROWS, rows)
    scale = HEAD_DIM ** -0.5
    grid = (B, rows, GRID_W, NA_HEADS, HEAD_DIM)
    qg, kg, vg = q.reshape(grid), k.reshape(grid), v.reshape(grid)
    col_start = np.clip(np.arange(GRID_W) - NA_COLS // 2, 0, GRID_W - NA_COLS)
    col_idx = col_start[:, None] + np.arange(NA_COLS)[None, :]
    col_off = col_idx - np.arange(GRID_W)[:, None] + (NA_COLS - 1)
    rpb_cols = rpb[:, :, col_off]

    def row_fn(i):
        rs = jnp.clip(i - kr // 2, 0, rows - kr)
        q_i = lax.dynamic_index_in_dim(qg, i, axis=1, keepdims=False)
        k_w = lax.dynamic_slice_in_dim(kg, rs, kr, axis=1)[:, :, col_idx]
        v_w = lax.dynamic_slice_in_dim(vg, rs, kr, axis=1)[:, :, col_idx]
        row_off = rs + jnp.arange(kr) - i + (NA_MAX_ROWS - 1)
        bias = jnp.transpose(rpb_cols[:, row_off], (0, 2, 1, 3)).astype(jnp.float32)
        s_w = jnp.einsum('bjhd,brjchd->bhjrc', q_i, k_w).astype(jnp.float32) * scale + bias[None]
        s_c = jnp.einsum('bjhd,bnhd->bhjn', q_i, k_ctx).astype(jnp.float32) * scale
        s = jnp.concatenate([s_w.reshape(B, NA_HEADS, GRID_W, kr * NA_COLS), s_c], axis=-1)
        p = jax.nn.softmax(s, axis=-1).astype(v.dtype)
        p_w = p[..., :kr * NA_COLS].reshape(B, NA_HEADS, GRID_W, kr, NA_COLS)
        o = (jnp.einsum('bhjrc,brjchd->bjhd', p_w, v_w)
             + jnp.einsum('bhjn,bnhd->bjhd', p[..., kr * NA_COLS:], v_ctx))
        return o

    out = lax.map(row_fn, jnp.arange(rows))
    return jnp.moveaxis(out, 0, 1).reshape(B, S, NA_HEADS * HEAD_DIM)

def window_attention(q, k, v, k_ctx, v_ctx, sink):
    B, S = q.shape[0], q.shape[1]
    G = WA_HEADS // WA_KV_HEADS
    nb = S // WA_BLOCK
    span = WA_BLOCK + 2 * WA_WINDOW
    scale = HEAD_DIM ** -0.5
    qb = q.reshape(B, nb, WA_BLOCK, WA_KV_HEADS, G, HEAD_DIM)
    pad = ((0, 0), (WA_WINDOW, WA_WINDOW), (0, 0), (0, 0))
    kp = jnp.pad(k, pad)
    vp = jnp.pad(v, pad)
    rel = (jnp.arange(span) - WA_WINDOW)[None, :] - jnp.arange(WA_BLOCK)[:, None]
    in_window = jnp.abs(rel) <= WA_WINDOW
    sink_b = sink.astype(jnp.float32).reshape(1, WA_KV_HEADS, G, 1, 1)

    def block_fn(n):
        start = n * WA_BLOCK
        q_n = lax.dynamic_index_in_dim(qb, n, axis=1, keepdims=False)
        k_n = lax.dynamic_slice_in_dim(kp, start, span, axis=1)
        v_n = lax.dynamic_slice_in_dim(vp, start, span, axis=1)
        kpos = start - WA_WINDOW + jnp.arange(span)
        valid = in_window & ((kpos >= 0) & (kpos < S))[None, :]
        s_w = jnp.einsum('bqkgd,bskd->bkgqs', q_n, k_n).astype(jnp.float32) * scale
        s_w = jnp.where(valid, s_w, -jnp.inf)
        s_c = jnp.einsum('bqkgd,bnkd->bkgqn', q_n, k_ctx).astype(jnp.float32) * scale
        p = sink_softmax(jnp.concatenate([s_w, s_c], axis=-1), sink_b).astype(v.dtype)
        o = (jnp.einsum('bkgqs,bskd->bqkgd', p[..., :span], v_n)
             + jnp.einsum('bkgqn,bnkd->bqkgd', p[..., span:], v_ctx))
        return o

    out = lax.map(block_fn, jnp.arange(nb))
    return jnp.moveaxis(out, 0, 1).reshape(B, S, WA_HEADS * HEAD_DIM)

def merge_branches(a_glu, a_gate, o_na, n_gate, o_wa, w_gate, merge,
                   conv_w, conv_b, cln_g, cln_b, w_proj_a, w_proj_b, w_proj_c, w_o):
    y_a = conv_branch(a_glu, a_gate, conv_w, conv_b, cln_g, cln_b, w_proj_a)
    y_b = (o_na * jax.nn.silu(n_gate)) @ w_proj_b
    y_c = (o_wa * jax.nn.silu(w_gate)) @ w_proj_c
    g_a, g_b, g_c = jnp.split(merge, 3, axis=-1)
    y = jax.nn.sigmoid(g_a) * y_a + jax.nn.sigmoid(g_b) * y_b + jax.nn.sigmoid(g_c) * y_c
    return y @ w_o

def context_kv(hc, w_in_l):
    st = SPLIT_STARTS
    nk, nv = jnp.split(hc @ w_in_l[:, st[3]:st[5]], 2, axis=-1)
    wk, wv = jnp.split(hc @ w_in_l[:, st[7]:st[9]], 2, axis=-1)
    return nk, nv, wk, wv

def first_inputs(seed: int = 0) -> dict:
    key = jax.random.key(seed)
    ks = jax.random.split(key, 24)
    L = DEPTH

    def nrm(k, shape, s):
        return jax.random.normal(k, shape, jnp.float32) * s

    return {
        'x': nrm(ks[0], (BATCH, SEQ, D_MODEL), 1.0),
        'c': nrm(ks[1], (BATCH, D_MODEL), 1.0),
        'ctx': nrm(ks[2], (BATCH, CTX_LEN, D_MODEL), 1.0),
        'c_ctx': nrm(ks[3], (D_MODEL,), 1.0),
        'norm_g': 1.0 + nrm(ks[4], (L, D_MODEL), 0.02),
        'w_ada': nrm(ks[5], (L, D_MODEL, 3 * D_MODEL), 0.5 * D_MODEL ** -0.5),
        'b_ada': nrm(ks[6], (L, 3 * D_MODEL), 0.02),
        'w_in': nrm(ks[7], (L, D_MODEL, D_IN), D_MODEL ** -0.5),
        'conv_w': nrm(ks[8], (L, CONV_K, D_CONV), CONV_K ** -0.5),
        'conv_b': nrm(ks[9], (L, D_CONV), 0.02),
        'cln_g': 1.0 + nrm(ks[10], (L, D_CONV), 0.02),
        'cln_b': nrm(ks[11], (L, D_CONV), 0.02),
        'w_proj_a': nrm(ks[12], (L, D_CONV, D_MODEL), D_CONV ** -0.5),
        'na_q_norm': 1.0 + nrm(ks[13], (L, HEAD_DIM), 0.02),
        'na_k_norm': 1.0 + nrm(ks[14], (L, HEAD_DIM), 0.02),
        'na_rpb': nrm(ks[15], (L, NA_HEADS, 2 * NA_MAX_ROWS - 1, 2 * NA_COLS - 1), 0.1),
        'w_proj_b': nrm(ks[16], (L, D_NA, D_MODEL), D_NA ** -0.5),
        'wa_q_norm': 1.0 + nrm(ks[17], (L, HEAD_DIM), 0.02),
        'wa_k_norm': 1.0 + nrm(ks[18], (L, HEAD_DIM), 0.02),
        'wa_sink': nrm(ks[19], (L, WA_HEADS), 1.0),
        'w_proj_c': nrm(ks[20], (L, D_WA, D_MODEL), D_WA ** -0.5),
        'w_o': nrm(ks[21], (L, D_MODEL, D_MODEL), D_MODEL ** -0.5),
    }

def first_block(x, c, ctx, c_ctx, norm_g, w_ada, b_ada, w_in, conv_w, conv_b, cln_g, cln_b,
              w_proj_a, na_q_norm, na_k_norm, na_rpb, w_proj_b, wa_q_norm, wa_k_norm,
              wa_sink, w_proj_c, w_o):
    B, S, _ = x.shape
    N = ctx.shape[1]
    G = WA_HEADS // WA_KV_HEADS
    t = jnp.arange(S)
    row_pos = t // GRID_W
    col_pos = t % GRID_W
    for l in range(DEPTH):
        update_ctx = l < DEPTH - 1
        mod = jax.nn.silu(c) @ w_ada[l] + b_ada[l]
        mod_c = jax.nn.silu(c_ctx) @ w_ada[l] + b_ada[l]
        shift, scale, gate = jnp.split(mod[:, None, :], 3, axis=-1)
        shift_c, scale_c, gate_c = jnp.split(mod_c[None, None, :], 3, axis=-1)
        h = rms_norm(x, norm_g[l]) * (1.0 + scale) + shift
        hc = rms_norm(ctx, norm_g[l]) * (1.0 + scale_c) + shift_c

        (a_glu, a_gate, nq, nk, nv, n_gate, wq, wk, wv, w_gate, merge) = jnp.split(
            h @ w_in[l], SPLIT_POINTS, axis=-1)
        if update_ctx:
            cp = jnp.split(hc @ w_in[l], SPLIT_POINTS, axis=-1)
            nck, ncv, wck, wcv = cp[3], cp[4], cp[7], cp[8]
        else:
            nck, ncv, wck, wcv = context_kv(hc, w_in[l])

        nk_c = rms_norm(split_heads(nck, NA_HEADS), na_k_norm[l])
        nv_c = split_heads(ncv, NA_HEADS)
        wk_c = rms_norm(split_heads(wck, WA_KV_HEADS), wa_k_norm[l])
        wv_c = split_heads(wcv, WA_KV_HEADS)

        o_na = neighbourhood_attention(
            rms_norm(split_heads(nq, NA_HEADS), na_q_norm[l]),
            rms_norm(split_heads(nk, NA_HEADS), na_k_norm[l]),
            split_heads(nv, NA_HEADS), nk_c, nv_c, na_rpb[l])
        o_wa = window_attention(
            axial_rope(rms_norm(split_heads(wq, WA_HEADS), wa_q_norm[l]), row_pos, col_pos),
            axial_rope(rms_norm(split_heads(wk, WA_KV_HEADS), wa_k_norm[l]), row_pos, col_pos),
            split_heads(wv, WA_KV_HEADS), wk_c, wv_c, wa_sink[l])
        y = merge_branches(a_glu, a_gate, o_na, n_gate, o_wa, w_gate, merge,
                           conv_w[l], conv_b[l], cln_g[l], cln_b[l],
                           w_proj_a[l], w_proj_b[l], w_proj_c[l], w_o[l])
        x_new = x + gate * y

        if update_ctx:
            (ac_glu, ac_gate, ncq, _, _, nc_gate, wcq, _, _, wc_gate, merge_c) = cp
            q_na_c = rms_norm(split_heads(ncq, NA_HEADS), na_q_norm[l])[:, :, :, None, :]
            oc_na = context_attention(q_na_c, nk_c, nv_c, None)
            q_wa_c = rms_norm(split_heads(wcq, WA_HEADS), wa_q_norm[l]).reshape(
                B, N, WA_KV_HEADS, G, HEAD_DIM)
            oc_wa = context_attention(q_wa_c, wk_c, wv_c, wa_sink[l].reshape(WA_KV_HEADS, G))
            yc = merge_branches(ac_glu, ac_gate, oc_na, nc_gate, oc_wa, wc_gate, merge_c,
                                conv_w[l], conv_b[l], cln_g[l], cln_b[l],
                                w_proj_a[l], w_proj_b[l], w_proj_c[l], w_o[l])
            ctx = ctx + gate_c * yc
        x = x_new
    return x


N_MIXERS = 2
LRU_WIDTH = 1280
LRU_BLOCKS = 10
LRU_BLOCK_W = LRU_WIDTH // LRU_BLOCKS
LRU_CONV = 4
LRU_C = 8.0
N_HEADS = 16
N_KV = 4
GROUP = N_HEADS // N_KV
N_BRANCH = 3
CMP_BLOCK = 32
CMP_STRIDE = 16
CMP_HIDDEN = 256
SEL_BLOCK = 64
N_SELECT = 8
WINDOW = 512
Q_BLOCK = 64
FORCED_BONUS = 1e4
NEG = -1e30
Q_COLS = N_HEADS * HEAD_DIM
KV_COLS = 2 * N_KV * HEAD_DIM
NSA_IN = Q_COLS + N_BRANCH * KV_COLS + N_BRANCH * N_HEADS
D_FF = 3072
FFN_CONV = 3


def rmsnorm(x, g):
    xf = x.astype(jnp.float32)
    y = xf * lax.rsqrt(jnp.mean(xf * xf, axis=-1, keepdims=True) + EPS)
    return (y * g.astype(jnp.float32)).astype(x.dtype)

def causal_dwconv(x, w, b):
    K, C = w.shape
    y = lax.conv_general_dilated(x, w[:, None, :].astype(x.dtype), window_strides=(1,),
                                 padding=[(K - 1, 0)], dimension_numbers=('NWC', 'WIO', 'NWC'),
                                 feature_group_count=C)
    return y + b.astype(x.dtype)

def alibi_slopes():
    s = 2.0 ** (-8.0 * np.arange(1, N_HEADS + 1) / N_HEADS)
    return jnp.asarray(s, dtype=jnp.float32).reshape(N_KV, GROUP)

def masked_softmax(s, m):
    return jax.nn.softmax(jnp.where(m, s, NEG), axis=-1)

def rglru_mixer(x, w_in, conv_w, conv_b, gate_w, gate_b, a_param, w_out):
    B, S, _ = x.shape
    y_br, x_br = jnp.split(x @ w_in, 2, axis=-1)
    y_br = jax.nn.gelu(y_br)
    xc = causal_dwconv(x_br, conv_w, conv_b)
    xb = xc.reshape(B, S, LRU_BLOCKS, LRU_BLOCK_W)
    g = jnp.einsum('bsnc,gncd->gbsnd', xb, gate_w).reshape(2, B, S, LRU_WIDTH)
    g = jax.nn.sigmoid(g.astype(jnp.float32) + gate_b.astype(jnp.float32)[:, None, None, :])
    r_gate, i_gate = g[0], g[1]
    log_a = -LRU_C * r_gate * jax.nn.softplus(-a_param.astype(jnp.float32))
    a = jnp.exp(log_a)
    mult = jnp.sqrt(-jnp.expm1(2.0 * log_a))
    bterm = mult * i_gate * xc.astype(jnp.float32)

    def combine(left, right):
        a1, b1 = left
        a2, b2 = right
        return a1 * a2, a2 * b1 + b2

    _, h = lax.associative_scan(combine, (a, bterm), axis=1)
    return (h.astype(x.dtype) * y_br) @ w_out

def nsa_mixer(x, w_in, cmp_pos, cmp_w1, cmp_b1, cmp_w2, w_out):
    B, S, _ = x.shape
    dt = x.dtype
    f32 = jnp.float32
    proj = x @ w_in
    q = proj[..., :Q_COLS].reshape(B, S, N_KV, GROUP, HEAD_DIM).transpose(0, 2, 3, 1, 4)
    q = q * (HEAD_DIM ** -0.5)
    kv = proj[..., Q_COLS:Q_COLS + N_BRANCH * KV_COLS].reshape(B, S, N_BRANCH, 2, N_KV, HEAD_DIM)
    kv = kv.transpose(2, 3, 0, 4, 1, 5)
    gates = jax.nn.sigmoid(proj[..., Q_COLS + N_BRANCH * KV_COLS:].astype(f32))
    gates = gates.reshape(B, S, N_BRANCH, N_KV, GROUP).transpose(2, 0, 3, 4, 1)
    slopes = alibi_slopes()

    n_cmp = (S - CMP_BLOCK) // CMP_STRIDE + 1
    cmp_start = jnp.arange(n_cmp) * CMP_STRIDE
    tok_idx = cmp_start[:, None] + jnp.arange(CMP_BLOCK)[None, :]

    def compress(t, pos, w1, b1, w2):
        blk = (t[:, :, tok_idx] + pos.astype(dt)).reshape(B, N_KV, n_cmp, CMP_BLOCK * HEAD_DIM)
        return jax.nn.gelu(blk @ w1 + b1.astype(dt)) @ w2

    k_cmp = compress(kv[0, 0], cmp_pos[0], cmp_w1[0], cmp_b1[0], cmp_w2[0])
    v_cmp = compress(kv[0, 1], cmp_pos[1], cmp_w1[1], cmp_b1[1], cmp_w2[1])
    cmp_end = cmp_start + CMP_BLOCK - 1
    cmp_center = cmp_start.astype(f32) + (CMP_BLOCK - 1) / 2.0

    n_sel = S // SEL_BLOCK
    n_top = min(N_SELECT, n_sel)
    sel_j = jnp.arange(n_sel)
    overlap = ((cmp_start[:, None] < (sel_j[None, :] + 1) * SEL_BLOCK) &
               (cmp_start[:, None] + CMP_BLOCK > sel_j[None, :] * SEL_BLOCK)).astype(f32)
    k_blocks = kv[1, 0].reshape(B, N_KV, n_sel, SEL_BLOCK, HEAD_DIM)
    v_blocks = kv[1, 1].reshape(B, N_KV, n_sel, SEL_BLOCK, HEAD_DIM)
    gather = jax.vmap(jax.vmap(lambda blk, ix: blk[ix]))

    pad = ((0, 0), (0, 0), (WINDOW, 0), (0, 0))
    k_win = jnp.pad(kv[2, 0], pad)
    v_win = jnp.pad(kv[2, 1], pad)

    def query_block(q0):
        qc = lax.dynamic_slice_in_dim(q, q0, Q_BLOCK, axis=3)
        gc = lax.dynamic_slice_in_dim(gates, q0, Q_BLOCK, axis=4)
        t = q0 + jnp.arange(Q_BLOCK)
        tf = t.astype(f32)
        sl = slopes[:, :, None, None]

        m_c = cmp_end[None, :] <= t[:, None]
        s = jnp.einsum('bgrqd,bgcd->bgrqc', qc, k_cmp, preferred_element_type=f32)
        s = s - sl * (tf[:, None] - cmp_center[None, :])
        p_cmp = masked_softmax(s, m_c) * m_c
        o_cmp = jnp.einsum('bgrqc,bgcd->bgrqd', p_cmp.astype(dt), v_cmp)

        imp = jnp.einsum('bgrqc,cj->bgqj', p_cmp, overlap)
        cur = t // SEL_BLOCK
        forced = (sel_j[None, :] == 0) | (sel_j[None, :] == cur[:, None]) | (sel_j[None, :] == cur[:, None] - 1)
        future = sel_j[None, :] > cur[:, None]
        score = jnp.where(forced, FORCED_BONUS, jnp.where(future, -1.0, imp))
        _, idx = lax.top_k(score, n_top)
        kg = gather(k_blocks, idx).reshape(B, N_KV, Q_BLOCK, n_top * SEL_BLOCK, HEAD_DIM)
        vg = gather(v_blocks, idx).reshape(B, N_KV, Q_BLOCK, n_top * SEL_BLOCK, HEAD_DIM)
        pos = (idx[..., None] * SEL_BLOCK + jnp.arange(SEL_BLOCK)).reshape(B, N_KV, Q_BLOCK, n_top * SEL_BLOCK)
        dist = (t[:, None] - pos)[:, :, None]
        s = jnp.einsum('bgrqd,bgqkd->bgrqk', qc, kg, preferred_element_type=f32)
        s = s - sl * dist.astype(f32)
        p = masked_softmax(s, dist >= 0)
        o_sel = jnp.einsum('bgrqk,bgqkd->bgrqd', p.astype(dt), vg)

        kw = lax.dynamic_slice_in_dim(k_win, q0, WINDOW + Q_BLOCK, axis=2)
        vw = lax.dynamic_slice_in_dim(v_win, q0, WINDOW + Q_BLOCK, axis=2)
        pos_w = q0 - WINDOW + jnp.arange(WINDOW + Q_BLOCK)
        dist_w = t[:, None] - pos_w[None, :]
        m_w = (dist_w >= 0) & (dist_w < WINDOW) & (pos_w[None, :] >= 0)
        s = jnp.einsum('bgrqd,bgkd->bgrqk', qc, kw, preferred_element_type=f32)
        s = s - sl * dist_w.astype(f32)
        p = masked_softmax(s, m_w)
        o_win = jnp.einsum('bgrqk,bgkd->bgrqd', p.astype(dt), vw)

        o = (gc[0][..., None] * o_cmp.astype(f32) + gc[1][..., None] * o_sel.astype(f32)
             + gc[2][..., None] * o_win.astype(f32)).astype(dt)
        return o.transpose(0, 3, 1, 2, 4).reshape(B, Q_BLOCK, Q_COLS)

    starts = jnp.arange(S // Q_BLOCK) * Q_BLOCK
    o = lax.map(query_block, starts)
    o = o.transpose(1, 0, 2, 3).reshape(B, S, Q_COLS)
    return o @ w_out

def conv_ffn(x, w_in, conv_w, conv_b, w_out):
    a, b = jnp.split(x @ w_in, 2, axis=-1)
    a = causal_dwconv(a, conv_w, conv_b)
    return (jax.nn.gelu(a) * b) @ w_out

def second_inputs(seed: int = 0) -> dict:
    key = jax.random.key(seed)
    ks = iter(jax.random.split(key, 32))
    n_a = len(range(0, DEPTH, N_MIXERS))
    n_b = len(range(1, DEPTH, N_MIXERS))

    def nrm(shape, scale):
        return jax.random.normal(next(ks), shape, jnp.float32) * scale

    def gain(shape):
        return 1.0 + nrm(shape, 0.05)

    x = nrm((BATCH, SEQ, D_MODEL), 1.0)
    lru_norm_g = gain((n_a, D_MODEL))
    lru_w_in = nrm((n_a, D_MODEL, 2 * LRU_WIDTH), D_MODEL ** -0.5)
    lru_conv_w = nrm((n_a, LRU_CONV, LRU_WIDTH), LRU_CONV ** -0.5)
    lru_conv_b = nrm((n_a, LRU_WIDTH), 0.02)
    lru_gate_w = nrm((n_a, 2, LRU_BLOCKS, LRU_BLOCK_W, LRU_BLOCK_W), LRU_BLOCK_W ** -0.5)
    lru_gate_b = nrm((n_a, 2, LRU_WIDTH), 0.1)
    a_c = jax.random.uniform(next(ks), (n_a, LRU_WIDTH), jnp.float32, 0.9, 0.999)
    s = a_c ** (1.0 / LRU_C)
    lru_a_param = jnp.log(s) - jnp.log1p(-s)
    lru_w_out = nrm((n_a, LRU_WIDTH, D_MODEL), LRU_WIDTH ** -0.5)
    nsa_norm_g = gain((n_b, D_MODEL))
    nsa_w_in = nrm((n_b, D_MODEL, NSA_IN), D_MODEL ** -0.5)
    nsa_cmp_pos = nrm((n_b, 2, CMP_BLOCK, HEAD_DIM), 0.1)
    nsa_cmp_w1 = nrm((n_b, 2, CMP_BLOCK * HEAD_DIM, CMP_HIDDEN), (CMP_BLOCK * HEAD_DIM) ** -0.5)
    nsa_cmp_b1 = nrm((n_b, 2, CMP_HIDDEN), 0.02)
    nsa_cmp_w2 = nrm((n_b, 2, CMP_HIDDEN, HEAD_DIM), CMP_HIDDEN ** -0.5)
    nsa_w_out = nrm((n_b, Q_COLS, D_MODEL), Q_COLS ** -0.5)
    ffn_norm_g = gain((DEPTH, D_MODEL))
    ffn_w_in = nrm((DEPTH, D_MODEL, 2 * D_FF), D_MODEL ** -0.5)
    ffn_conv_w = nrm((DEPTH, FFN_CONV, D_FF), FFN_CONV ** -0.5)
    ffn_conv_b = nrm((DEPTH, D_FF), 0.02)
    ffn_w_out = nrm((DEPTH, D_FF, D_MODEL), D_FF ** -0.5)
    final_norm_g = gain((D_MODEL,))
    return {"x": x, "lru_norm_g": lru_norm_g, "lru_w_in": lru_w_in, "lru_conv_w": lru_conv_w,
            "lru_conv_b": lru_conv_b, "lru_gate_w": lru_gate_w, "lru_gate_b": lru_gate_b,
            "lru_a_param": lru_a_param, "lru_w_out": lru_w_out, "nsa_norm_g": nsa_norm_g,
            "nsa_w_in": nsa_w_in, "nsa_cmp_pos": nsa_cmp_pos, "nsa_cmp_w1": nsa_cmp_w1,
            "nsa_cmp_b1": nsa_cmp_b1, "nsa_cmp_w2": nsa_cmp_w2, "nsa_w_out": nsa_w_out,
            "ffn_norm_g": ffn_norm_g, "ffn_w_in": ffn_w_in, "ffn_conv_w": ffn_conv_w,
            "ffn_conv_b": ffn_conv_b, "ffn_w_out": ffn_w_out, "final_norm_g": final_norm_g}

def second_block(x, lru_norm_g, lru_w_in, lru_conv_w, lru_conv_b, lru_gate_w, lru_gate_b,
              lru_a_param, lru_w_out, nsa_norm_g, nsa_w_in, nsa_cmp_pos, nsa_cmp_w1,
              nsa_cmp_b1, nsa_cmp_w2, nsa_w_out, ffn_norm_g, ffn_w_in, ffn_conv_w,
              ffn_conv_b, ffn_w_out, final_norm_g):
    h = x
    for layer in range(DEPTH):
        mixer, j = layer % N_MIXERS, layer // N_MIXERS
        if mixer == 0:
            h = h + rglru_mixer(rmsnorm(h, lru_norm_g[j]), lru_w_in[j], lru_conv_w[j], lru_conv_b[j],
                                lru_gate_w[j], lru_gate_b[j], lru_a_param[j], lru_w_out[j])
        else:
            h = h + nsa_mixer(rmsnorm(h, nsa_norm_g[j]), nsa_w_in[j], nsa_cmp_pos[j], nsa_cmp_w1[j],
                              nsa_cmp_b1[j], nsa_cmp_w2[j], nsa_w_out[j])
        h = h + conv_ffn(rmsnorm(h, ffn_norm_g[layer]), ffn_w_in[layer], ffn_conv_w[layer],
                         ffn_conv_b[layer], ffn_w_out[layer])
    return rmsnorm(h, final_norm_g)


def setup_inputs(seed=0):
    out = dict(first_inputs(seed))
    for name, value in second_inputs(seed + 1).items():
        if name != "x":
            out[name + "_2"] = value
    return out


def reference(
    x, c, ctx, c_ctx, norm_g, w_ada, b_ada, w_in, conv_w, conv_b, cln_g, cln_b, w_proj_a,
    na_q_norm, na_k_norm, na_rpb, w_proj_b, wa_q_norm, wa_k_norm, wa_sink, w_proj_c, w_o,
    lru_norm_g_2, lru_w_in_2, lru_conv_w_2, lru_conv_b_2, lru_gate_w_2, lru_gate_b_2,
    lru_a_param_2, lru_w_out_2, nsa_norm_g_2, nsa_w_in_2, nsa_cmp_pos_2, nsa_cmp_w1_2,
    nsa_cmp_b1_2, nsa_cmp_w2_2, nsa_w_out_2, ffn_norm_g_2, ffn_w_in_2, ffn_conv_w_2,
    ffn_conv_b_2, ffn_w_out_2, final_norm_g_2,
):
    x = first_block(
        x, c, ctx, c_ctx, norm_g, w_ada, b_ada, w_in, conv_w, conv_b, cln_g, cln_b, w_proj_a,
        na_q_norm, na_k_norm, na_rpb, w_proj_b, wa_q_norm, wa_k_norm, wa_sink, w_proj_c, w_o,
    )
    return second_block(
        x, lru_norm_g_2, lru_w_in_2, lru_conv_w_2, lru_conv_b_2, lru_gate_w_2, lru_gate_b_2,
        lru_a_param_2, lru_w_out_2, nsa_norm_g_2, nsa_w_in_2, nsa_cmp_pos_2, nsa_cmp_w1_2,
        nsa_cmp_b1_2, nsa_cmp_w2_2, nsa_w_out_2, ffn_norm_g_2, ffn_w_in_2, ffn_conv_w_2,
        ffn_conv_b_2, ffn_w_out_2, final_norm_g_2,
    )


_drawn_inputs = setup_inputs


def setup_inputs(seed=0):
    import zlib

    import numpy as np

    out = dict(_drawn_inputs(seed))
    spreads = {}
    factors = {'norm_g': 8.0,
     'b_ada': 3.615,
     'conv_b': 8.0,
     'cln_g': 8.0,
     'cln_b': 8.0,
     'na_q_norm': 8.0,
     'na_k_norm': 8.0,
     'na_rpb': 8.0,
     'wa_q_norm': 8.0,
     'wa_k_norm': 8.0,
     'wa_sink': 8.0,
     'lru_gate_b_2': 180.096,
     'nsa_cmp_b1_2': 64.0,
     'ffn_conv_b_2': 30.648,
     'lru_norm_g_2': 64.0,
     'lru_conv_b_2': 64.0,
     'lru_gate_w_2': 47.424,
     'lru_a_param_2': 62.04,
     'nsa_norm_g_2': 8.0,
     'nsa_w_in_2': 3.337,
     'nsa_cmp_pos_2': 8.0,
     'nsa_cmp_w1_2': 5.437,
     'nsa_cmp_w2_2': 4.496,
     'nsa_w_out_2': 3.132,
     'ffn_norm_g_2': 8.0,
     'lru_w_in_2': 8.0,
     'lru_conv_w_2': 8.0,
     'lru_w_out_2': 8.0}
    for name, (base, spread) in spreads.items():
        noise = np.random.default_rng([zlib.crc32(name.encode()), seed]).standard_normal(out[name].shape)
        drawn = base * np.exp(spread * noise) if base else spread * noise
        out[name] = jnp.asarray(drawn.astype(out[name].dtype))
    for name, factor in factors.items():
        out[name] = (out[name] * factor).astype(out[name].dtype)
    return out
```

```python
import math
from contextlib import ExitStack

import numpy as np
import concourse.bass as bass
from concourse import mybir

F32 = mybir.dt.float32
F32R = mybir.dt.float32r
ALU = mybir.AluOpType
ACT = mybir.ActivationFunctionType
AX = mybir.AxisListType

S = 512
NCTX = 256
NT = S + NCTX
EPS = 1e-6
NEG = -1e30
FAR = 1e33
NRAW = 4
NSPL = 3
ENGINES = ("tensor", "vector", "scalar", "gpsimd", "sync")

SM_PARTS = [("cc", 16)]
for _l in range(2):
    SM_PARTS += [(f"norm_g{_l}", 8), (f"b_ada{_l}", 24), (f"conv_w{_l}", 124), (f"conv_b{_l}", 4),
                 (f"cln_g{_l}", 4), (f"cln_b{_l}", 4), (f"na_q{_l}", 1), (f"na_k{_l}", 1),
                 (f"wa_q{_l}", 1), (f"wa_k{_l}", 1), (f"sink{_l}", 8)]
SM_PARTS += [("lru_norm", 8), ("lru_conv_w", 40), ("lru_conv_b", 10), ("gate_b", 20), ("a_param", 10),
             ("nsa_norm", 8), ("cmp_pos", 32), ("cmp_b1", 4), ("cmp_w2", 256), ("ffn_norm0", 8),
             ("ffn_norm1", 8), ("ffn_cw0", 72), ("ffn_cw1", 72), ("ffn_cb0", 24), ("ffn_cb1", 24),
             ("final_g", 8)]
SM_AT = {}
_n = 0
for _k, _w in SM_PARTS:
    SM_AT[_k] = (_n, _w)
    _n += _w
SM_N = _n
SM_1 = SM_AT["lru_norm"][0]


class Call:

    def matmul(self, *a, **k): return lambda e: e.matmul(*a, **k)
    def transpose(self, *a, **k): return lambda e: e.transpose(*a, **k)
    def activation(self, *a, **k): return lambda e: e.activation(*a, **k)
    def tensor_copy(self, *a, **k): return lambda e: e.tensor_copy(*a, **k)
    def tensor_tensor(self, *a, **k): return lambda e: e.tensor_tensor(*a, **k)
    def tensor_scalar(self, *a, **k): return lambda e: e.tensor_scalar(*a, **k)
    def scalar_tensor_tensor(self, *a, **k): return lambda e: e.scalar_tensor_tensor(*a, **k)
    def tensor_tensor_scan(self, *a, **k): return lambda e: e.tensor_tensor_scan(*a, **k)
    def tensor_reduce(self, *a, **k): return lambda e: e.tensor_reduce(*a, **k)
    def reciprocal(self, *a, **k): return lambda e: e.reciprocal(*a, **k)
    def memset(self, *a, **k): return lambda e: e.memset(*a, **k)


CALL = Call()


class Program:

    def __init__(self):
        self.queue = {e: [] for e in ENGINES}
        self.count = {e: 0 for e in ENGINES}
        self.dma_count = {}

    def op(self, engine, fn, *waits, inc=True):
        self.queue[engine].append((flat(waits), fn(CALL), engine if inc else None, 1))
        if inc:
            self.count[engine] += 1
            return (engine, self.count[engine])
        return None

    def dma(self, engine, sem, dst, src, *waits):
        self.dma_count[sem] = self.dma_count.get(sem, 0) + 16
        self.queue[engine].append((flat(waits), lambda e: e.dma_start(dst, src), sem, 16))
        return (sem, self.dma_count[sem])

    def now(self):
        return [(e, c) for e, c in self.count.items() if c]

    def barrier(self):
        now = self.now()
        for e in ENGINES:
            self.queue[e].append((now, None, None, 0))
        return now

    def emit(self, nc, sems):
        with nc.Block() as block:
            for name in ENGINES:
                def body(e, name=name):
                    seen = {}
                    for waits, fn, sem, step in self.queue[name]:
                        for s, v in waits:
                            if seen.get(s, 0) < v:
                                e.wait_ge(sems[s], v)
                                seen[s] = v
                        if fn is not None:
                            ins = fn(e)
                            if sem is not None:
                                ins.then_inc(sems[sem], step)
                enter = {"tensor": block.tensor, "vector": block.vector, "scalar": block.scalar,
                                 "gpsimd": block.gpsimd, "sync": block.sync}[name]
                enter(body)


def flat(waits):
    best = {}
    stack = [waits]
    while stack:
        w = stack.pop()
        if w is None:
            continue
        if isinstance(w, tuple) and len(w) == 2 and isinstance(w[0], str):
            best[w[0]] = max(best.get(w[0], 0), w[1])
        else:
            stack.extend(w)
    return sorted(best.items())


class Ring:

    def __init__(self, items):
        self.items = items
        self.free = [[] for _ in items]
        self.at = -1

    def take(self):
        self.at = (self.at + 1) % len(self.items)
        return self.at, self.items[self.at], self.free[self.at]

    def release(self, slot, *tokens):
        self.free[slot] = list(tokens)


def build(nc, t, out, order, sems_out):
    P = Program()
    ctx = ExitStack()
    log = []

    def sb(name, shape, dt=F32, stack=ctx):
        return stack.enter_context(nc.sbuf_tensor(name, shape, dt))

    with ctx:
        X = sb("X", [128, 8, S])
        RAW = [sb(f"RAW{i}", [128, 1024]) for i in range(NRAW)]
        WH = [sb(f"WH{i}", [128, 1024], F32R) for i in range(NSPL)]
        WL = [sb(f"WL{i}", [128, 1024], F32R) for i in range(NSPL)]
        SM = sb("SM", [128, SM_N - SM_1])
        CO = sb("CO", [128, 512])
        MOD = sb("MOD", [128, 24, 2])
        AB = sb("AB", [128, 8, 2])
        EPSC = sb("EPSC", [128, 1])
        STAT = sb("STAT", [128, 8, 8])
        tmps = [sb(f"T{i}", [128, NT]) for i in range(6)]
        PS = ctx.enter_context(nc.psum_tensor("PS", [128, 4, 1024], F32))
        sems = sems_out

        ident = CO[:, 0:128]
        ones = CO[:, 128:256]
        bones = CO[:, 256:384]
        rmat = CO[:, 384:512]

        def smc(a, b):
            return SMA[:, a:b] if a < SM_1 else SM[:, a - SM_1:b - SM_1]

        def sm(name, a=0, n=None):
            o, w = SM_AT[name]
            return smc(o + a, o + a + (w - a if n is None else n))

        def V(fn, *w): return P.op("vector", fn, *w)
        def A(fn, *w): return P.op("scalar", fn, *w)
        def G(fn, *w): return P.op("gpsimd", fn, *w)
        def MM(fn, *w, inc=True): return P.op("tensor", fn, *w, inc=inc)

        pairs = Ring([PS[:, i, :] for i in range(4)])
        tmp = Ring(tmps)
        stat = Ring([STAT[:, i, :] for i in range(8)])

        st = {"dma": 0, "split": 0, "spl": 0, "use": 0}
        raw_free = {}
        raw_ready = {}
        split_ready = {}
        spl_free = {}
        spl_slot = {}

        def pump_dma():
            while st["dma"] < len(order):
                j = st["dma"]
                if j >= NRAW and (j - NRAW) not in raw_free:
                    return
                name, idx, c0, n, _ = order[j]
                raw_ready[j] = P.dma("sync", f"w{j % NRAW}", RAW[j % NRAW][:, 0:n], t[name][idx, :, c0:c0 + n],
                                     raw_free.get(j - NRAW))
                st["dma"] += 1

        def split_next():
            j = st["split"]
            name, idx, c0, n, split = order[j]
            if split:
                k = st["spl"]
                slot = k % NSPL
                wait = spl_free.get(k - NSPL)
                src = RAW[j % NRAW][:, 0:n]
                hi, lo = WH[slot][:, 0:n], WL[slot][:, 0:n]
                a = A(lambda e: e.activation(hi, src, ACT.Copy), raw_ready[j], wait)
                b = V(lambda e: e.tensor_tensor(lo, src, hi.bitcast(F32), ALU.subtract), a)
                raw_free[j] = [a, b]
                split_ready[j] = b
                spl_slot[j] = (slot, k)
                st["spl"] += 1
                st["split"] += 1
                pump_dma()
            else:
                st["split"] += 1

        def chunk(name, idx, c0, n, split=True):
            log.append((name, idx, c0, n, split))
            j = st["use"]
            st["use"] += 1
            if not order:
                return (WH[0][:, 0:n], WL[0][:, 0:n]) if split else RAW[0][:, 0:n], None, j
            assert order[j] == (name, idx, c0, n, split)
            pump_dma()
            while st["split"] <= j or (st["split"] < len(order) and order[st["split"]][4]
                                       and st["split"] <= j + NSPL - 1
                                       and st["spl"] - NSPL < spl_slot.get(j, (0, 1 << 30))[1]
                                       and raw_ready.get(st["split"]) is not None):
                split_next()
            if split:
                slot = spl_slot[j][0]
                return (WH[slot][:, 0:n], WL[slot][:, 0:n]), split_ready[j], j
            return RAW[j % NRAW][:, 0:n], raw_ready[j], j

        def chunk_done(j, tok):
            if not order:
                return
            if order[j][4]:
                spl_free[spl_slot[j][1]] = tok
            else:
                raw_free[j] = tok
                pump_dma()

        def linear(parts, rhs, ranges, waits):
            slot, ps, free = pairs.take()
            total = sum(len(ks) for _, ks in parts)
            seen = 0
            for args, ks in parts:
                (hi, lo), ready, j = chunk(*args)
                for i, k in enumerate(ks):
                    xh, xl = rhs(k)
                    for a, n, c in ranges:
                        for q, (w, x) in enumerate(((hi, xh), (hi, xl), (lo, xh))):
                            last = q == 2 and k == ks[-1] and (a, n, c) == ranges[-1]
                            tok = MM(lambda e, w=w, x=x, i=i, a=a, n=n, c=c, s=(seen == 0 and q == 0),
                                     z=(seen == total - 1 and q == 2):
                                     e.matmul(ps[:, c:c + n], w[:, 128 * i:128 * i + 128], x[:, a:a + n],
                                              start=s, stop=z),
                                     ready, waits, free, inc=last)
                    seen += 1
                chunk_done(j, tok)
            return slot, ps, tok

        R768 = [(0, 512, 0), (512, 256, 512)]
        R512 = [(0, 512, 0)]

        def split_into(hi, lo, src, *w):
            a = A(lambda e: e.activation(hi, src, ACT.Copy), *w)
            b = V(lambda e: e.tensor_tensor(lo, src, hi.bitcast(F32), ALU.subtract), a, *w)
            return [a, b]

        CS = sb("CS", [128, 16])
        both = ExitStack()
        XC2 = sb("XC2", [128, 8, NCTX], F32, both)
        SMA = sb("SMA", [128, SM_1], F32, both)

        def xa(k, a0, n):
            return X[:, k, a0:a0 + n] if a0 < S else XC2[:, k, a0 - S:a0 - S + n]

        c_sm = [P.dma("sync", "sm", SMA[:, :], t["sm"][:, 0:SM_1]), P.dma("sync", "sm2", SM[:, :], t["sm"][:, SM_1:])]
        c_co = P.dma("sync", "co", CO[:, :], t["co"][:, :])
        g_eps = G(lambda e: e.memset(EPSC[:, :], EPS))
        pump_dma()

        x_done = []
        with ExitStack() as ph:
            XT = [sb(f"XT{i}", [128, 1024], F32, ph) for i in range(3)]
            xr = Ring(XT)
            for i in range(6):
                xs, xt, free = xr.take()
                src = t["x"][128 * i:128 * i + 128, :] if i < 4 else t["ctx"][128 * (i - 4):128 * (i - 4) + 128, :]
                d = P.dma("scalar", f"xt{xs}", xt[:, :], src, free)
                slot, ps, pf = pairs.take()
                for k in range(8):
                    tok = MM(lambda e, k=k, xt=xt, ps=ps: e.transpose(ps[:, 128 * k:128 * k + 128], xt[:, 128 * k:128 * k + 128], ident),
                             d, c_co, pf, inc=(k == 7))
                xr.release(xs, tok)
                v = V(lambda e, i=i, ps=ps: e.tensor_copy(X[:, :, 128 * i:128 * i + 128] if i < 4 else XC2[:, :, 128 * i - S:128 * i - S + 128], ps.rearrange("p (k n) -> p k n", k=8)), tok)
                pairs.release(slot, v)
                x_done.append(v)
        cs = A(lambda e: e.activation(CS[:, :], sm("cc"), ACT.Silu), c_sm)
        P.barrier()

        def rsqrt(ps, n, scale, w, *out_free):
            ysl, y, yf = tmp.take()
            vsl, v, vf = tmp.take()
            asl, a, af = tmp.take()
            d = V(lambda e: e.tensor_scalar(v[:, 0:n], ps[:, 0:n], scale, EPS, ALU.mult, ALU.add), w, vf)
            l = A(lambda e: e.activation(y[:, 0:n], v[:, 0:n], ACT.Ln), d, yf)
            l = A(lambda e: e.activation(y[:, 0:n], y[:, 0:n], ACT.Exp, scale=-0.5), l)
            x = V(lambda e: e.scalar_tensor_tensor(a[:, 0:n], y[:, 0:n], -0.5, y[:, 0:n], ALU.mult, ALU.mult), l, af)
            x = V(lambda e: e.tensor_tensor(a[:, 0:n], a[:, 0:n], v[:, 0:n], ALU.mult), x)
            x = V(lambda e: e.scalar_tensor_tensor(y[:, 0:n], a[:, 0:n], 1.5, y[:, 0:n], ALU.add, ALU.mult), x)
            tmp.release(vsl, x)
            tmp.release(asl, x)
            return ysl, y, x, d

        def rms(ntok, ranges, waits, hh, hl, scale_of, bias_of):
            slot, ps, free = pairs.take()
            for k in range(8):
                ts, sq, tf = tmp.take()
                a = [A(lambda e, k=k, sq=sq, a0=a0, n=n: e.activation(sq[:, a0:a0 + n], xa(k, a0, n), ACT.Square), waits, tf) for a0, n, c in ranges]
                for a0, n, c in ranges:
                    tok = MM(lambda e, k=k, sq=sq, a0=a0, n=n, c=c: e.matmul(ps[:, c:c + n], ones, sq[:, a0:a0 + n], start=(k == 0), stop=(k == 7)),
                             a, free, inc=((a0, n, c) == ranges[-1]))
                tmp.release(ts, tok)
            rs, ri, r, l = rsqrt(ps, ntok, 1.0 / 1024, tok)
            pairs.release(slot, l)
            done = []
            for k in range(8):
                ts, h, tf = tmp.take()
                if h is ri:
                    ts, h, tf = tmp.take()
                a = [V(lambda e, k=k, h=h, a0=a0, n=n: e.tensor_tensor(h[:, a0:a0 + n], xa(k, a0, n), ri[:, a0:a0 + n], ALU.mult), r, tf) for a0, n, c in ranges]
                bs = []
                for q, (a0, n, c) in enumerate(ranges):
                    bi = bias_of(k, q)
                    if bi is None:
                        bs.append(V(lambda e, k=k, q=q, h=h, a0=a0, n=n: e.tensor_scalar(h[:, a0:a0 + n], h[:, a0:a0 + n], scale_of(k, q), None, ALU.mult), a))
                    else:
                        bs.append(V(lambda e, k=k, q=q, h=h, a0=a0, n=n, bi=bi: e.tensor_scalar(h[:, a0:a0 + n], h[:, a0:a0 + n], scale_of(k, q), bi, ALU.mult, ALU.add), a))
                s = split_into(hh[:, k, 0:ntok], hl[:, k, 0:ntok], h[:, 0:ntok], bs)
                tmp.release(ts, s)
                done.append(s)
            tmp.release(rs, done)
            return done

        def attention(steps):
            sring = Ring([PS[:, 0, :], PS[:, 1, :]])
            tring = Ring([PS[:, 2, :], PS[:, 3, :]])
            for i in range(2):
                sring.free[i] = pairs.free[i]
                tring.free[i] = pairs.free[2 + i]
            prob = Ring(tmps[0:2])
            prot = Ring(tmps[2:4])
            for i in range(2):
                prob.free[i] = tmp.free[i]
                prot.free[i] = tmp.free[2 + i]

            def first(s):
                slot, ps, free = sring.take()
                a, b = s["a"], s["b"]
                for kk, c, n in s["ks"]:
                    tok = MM(lambda e, ps=ps, kk=kk, c=c, n=n: e.matmul(ps[:, c:c + n], s["q"], kk, start=True, stop=True),
                             free, s["wait"])
                if s["bias"] is not None:
                    tok = s["bias"](ps, tok)
                ss, sv, sf = stat.take()
                m = V(lambda e: e.tensor_reduce(sv[:, 0:1], ps[:, a:b], AX.X, ALU.max, negate=True), tok, sf)
                es = None
                if s["sink"] is not None:
                    m = V(lambda e: e.scalar_tensor_tensor(sv[:, 0:1], s["sink"], -1.0, sv[:, 0:1], ALU.mult, ALU.min), m)
                    es = A(lambda e: e.activation(sv[:, 1:2], s["sink"], ACT.Exp, bias=sv[:, 0:1]), m)
                pslot, pr, pf = prob.take()
                x = A(lambda e: e.activation(pr[:, a:b], ps[:, a:b], ACT.Exp, bias=sv[:, 0:1]), m, pf)
                sring.release(slot, x, m)
                s.update(ss=ss, sv=sv, es=es, pslot=pslot, pr=pr, x=x)

            def second(s):
                slot, ps, free = tring.take()
                nb = (s["b"] - s["a"]) // 128
                for i in range(nb):
                    c = s["a"] + 128 * i
                    tok = MM(lambda e, i=i, c=c: e.transpose(ps[:, 128 * i:128 * i + 128], s["pr"][:, c:c + 128], ident),
                             free, s["x"], inc=(i == nb - 1))
                prob.release(s["pslot"], tok)
                qslot, pt, qf = prot.take()
                n = 128 * nb
                if s["act"]:
                    y = A(lambda e: e.activation(pt[:, 0:n], ps[:, 0:n], ACT.Copy), tok, qf)
                else:
                    y = V(lambda e: e.tensor_copy(pt[:, 0:n], ps[:, 0:n]), tok, qf)
                s.update(tslot=slot, tps=ps, qslot=qslot, pt=pt, y=y)

            def third(s):
                ps, pt = s["tps"], s["pt"]
                n = len(s["vs"])
                for i, v in enumerate(s["vs"]):
                    tok = MM(lambda e, i=i, v=v: e.matmul(ps[:, 768:833], pt[:, 128 * i:128 * i + 128], v, start=(i == 0), stop=(i == n - 1)),
                             s["y"], s["wait"], inc=(i == n - 1))
                prot.release(s["qslot"], tok)
                ss, sv = s["ss"], s["sv"]
                if s["es"] is not None:
                    d = V(lambda e: e.tensor_tensor(sv[:, 2:3], ps[:, 832:833], sv[:, 1:2], ALU.add), tok, s["es"])
                    d = V(lambda e: e.reciprocal(sv[:, 3:4], sv[:, 2:3]), d)
                else:
                    d = V(lambda e: e.reciprocal(sv[:, 3:4], ps[:, 832:833]), tok)
                o = s["fin"](ps[:, 768:832], sv[:, 3:4], d)
                stat.release(ss, o)
                tring.release(s["tslot"], o)
                if s["post"] is not None:
                    s["post"](tring, s["tslot"])

            n = len(steps)
            for i in range(n + 2):
                if i < n:
                    first(steps[i])
                if 1 <= i <= n:
                    second(steps[i - 1])
                if i >= 2:
                    third(steps[i - 2])
            for i in range(2):
                pairs.free[i] = sring.free[i]
                pairs.free[2 + i] = tring.free[i]
                tmp.free[i] = prob.free[i]
                tmp.free[2 + i] = prot.free[i]

        for L in range(2):
            lay = ExitStack()
            ntk = NT if L == 0 else S
            rx = R768 if L == 0 else R512
            slot, ps, free = pairs.take()
            for m in range(24):
                w, ready, j = chunk(f"w_ada{L}", m, 0, 1024, False)
                for k in range(8):
                    tok = MM(lambda e, m=m, k=k, w=w, ps=ps: e.matmul(ps[:, 2 * m:2 * m + 2], w[:, 128 * k:128 * k + 128], CS[:, 2 * k:2 * k + 2], start=(k == 0), stop=(k == 7)),
                             ready, cs, free, inc=(k == 7))
                chunk_done(j, tok)
            md = []
            for q in range(2):
                md.append(V(lambda e, q=q, ps=ps: e.tensor_tensor(MOD[:, :, q], ps[:, q:48:2], sm(f"b_ada{L}"), ALU.add), tok, c_sm, P.now()))
            pairs.release(slot, md)
            for q in range(2):
                a = V(lambda e, q=q: e.scalar_tensor_tensor(AB[:, :, q], MOD[:, 8:16, q], 1.0, sm(f"norm_g{L}"), ALU.add, ALU.mult), md)
            Hh = sb(f"Hh{L}", [128, 8, NT], F32R, lay)
            Hl = sb(f"Hl{L}", [128, 8, NT], F32R, lay)
            hd = rms(NT, R768, [a, x_done], Hh, Hl, lambda k, q: AB[:, k, q:q + 1], lambda k, q: MOD[:, k, q:q + 1])
            Y = sb(f"Y{L}", [128, 8, ntk], F32, lay)
            ydone = [None] * 8

            def win(col, ranges, L=L, hd=hd, Hh=Hh, Hl=Hl):
                return linear([((f"w_in{L}", col // 128, 0, 1024), list(range(8)))],
                              lambda k: (Hh[:, k, :], Hl[:, k, :]), ranges, hd)

            def merge(branch, wname, Gh, Gl, gdone, L=L, ntk=ntk, rx=rx, Y=Y, ydone=ydone, win=win):
                for m in range(8):
                    s1, p1, t1 = win(4864 + 1024 * branch + 128 * m, rx)
                    ts, sg, tf = tmp.take()
                    g = A(lambda e, sg=sg, p1=p1: e.activation(sg[:, 0:ntk], p1[:, 0:ntk], ACT.Sigmoid), t1, tf)
                    pairs.release(s1, g)
                    s2, p2, t2 = linear([((f"{wname}{L}", m, 0, 512), [0, 1, 2, 3])],
                                        lambda k: (Gh[:, k, :], Gl[:, k, :]), rx, gdone)
                    if branch == 0:
                        y = V(lambda e, m=m, sg=sg, p2=p2: e.tensor_tensor(Y[:, m, :], sg[:, 0:ntk], p2[:, 0:ntk], ALU.mult), t2, g)
                        pairs.release(s2, y)
                    else:
                        y = V(lambda e, sg=sg, p2=p2: e.tensor_tensor(sg[:, 0:ntk], sg[:, 0:ntk], p2[:, 0:ntk], ALU.mult), t2, g)
                        pairs.release(s2, y)
                        y = V(lambda e, m=m, sg=sg: e.tensor_tensor(Y[:, m, :], Y[:, m, :], sg[:, 0:ntk], ALU.add), y, ydone[m])
                    tmp.release(ts, y)
                    ydone[m] = y

            with ExitStack() as ph:
                W2 = NT + 60
                AP_ = [sb(f"AP{L}{i}", [128, W2], F32, ph) for i in range(2)]
                C = sb(f"C{L}", [128, 4, ntk], F32, ph)
                Gh = sb(f"CGh{L}", [128, 4, ntk], F32R, ph)
                Gl = sb(f"CGl{L}", [128, 4, ntk], F32R, ph)
                segs = [(0, 512, 15)] + ([(512, 256, 15 + 512 + 30)] if L == 0 else [])
                z = [G(lambda e, ap=ap: e.memset(ap[:, :], 0.0), P.now() if L else None) for ap in AP_]
                apr = Ring(AP_)
                cd = []
                cw = SM_AT[f"conv_w{L}"][0]
                for m in range(4):
                    s1, p1, t1 = win(512 + 128 * m, rx)
                    ts, sg, tf = tmp.take()
                    g = A(lambda e, sg=sg, p1=p1: e.activation(sg[:, 0:ntk], p1[:, 0:ntk], ACT.Sigmoid), t1, tf)
                    pairs.release(s1, g)
                    s2, p2, t2 = win(128 * m, rx)
                    aslot, ap, af = apr.take()
                    ys = [V(lambda e, ap=ap, sg=sg, p2=p2, a0=a0, n=n, o=o: e.tensor_tensor(ap[:, o:o + n], sg[:, a0:a0 + n], p2[:, a0:a0 + n], ALU.mult), t2, g, af, z)
                          for a0, n, o in segs]
                    pairs.release(s2, ys)
                    tmp.release(ts, ys)
                    last = []
                    for a0, n, o in segs:
                        y = V(lambda e, m=m, ap=ap, a0=a0, n=n, o=o: e.tensor_scalar(C[:, m, a0:a0 + n], ap[:, o - 15:o - 15 + n], smc(cw + 31 * m, cw + 31 * m + 1), sm(f"conv_b{L}", m, 1), ALU.mult, ALU.add), ys)
                        for k in range(1, 31):
                            y = V(lambda e, m=m, k=k, ap=ap, a0=a0, n=n, o=o: e.scalar_tensor_tensor(C[:, m, a0:a0 + n], ap[:, o - 15 + k:o - 15 + k + n], smc(cw + 31 * m + k, cw + 31 * m + k + 1), C[:, m, a0:a0 + n], ALU.mult, ALU.add), y)
                        last.append(y)
                    apr.release(aslot, last)
                    cd.append(last)
                s1, p1, pf = pairs.take()
                for m in range(4):
                    for a0, n, c in rx:
                        tok = MM(lambda e, m=m, a0=a0, n=n, c=c, p1=p1: e.matmul(p1[:, c:c + n], ones, C[:, m, a0:a0 + n], start=(m == 0), stop=(m == 3)), cd[m], pf)
                cs2 = []
                for m in range(4):
                    cs2.append(V(lambda e, m=m, p1=p1: e.scalar_tensor_tensor(C[:, m, :], p1[:, 0:ntk], -1.0 / 512, C[:, m, :], ALU.mult, ALU.add), tok))
                pairs.release(s1, cs2)
                s1, p1, pf = pairs.take()
                for m in range(4):
                    ts, sq, tf = tmp.take()
                    a = A(lambda e, m=m, sq=sq: e.activation(sq[:, 0:ntk], C[:, m, :], ACT.Square), cs2[m], tf)
                    for a0, n, c in rx:
                        tok = MM(lambda e, m=m, sq=sq, a0=a0, n=n, c=c, p1=p1: e.matmul(p1[:, c:c + n], ones, sq[:, a0:a0 + n], start=(m == 0), stop=(m == 3)), a, pf)
                    tmp.release(ts, tok)
                rs, ri, r, l = rsqrt(p1, ntk, 1.0 / 512, tok)
                pairs.release(s1, l)
                lnd = []
                for m in range(4):
                    y = V(lambda e, m=m: e.tensor_tensor(C[:, m, :], C[:, m, :], ri[:, 0:ntk], ALU.mult), r)
                    lnd.append(A(lambda e, m=m: e.activation(C[:, m, :], C[:, m, :], ACT.Silu, bias=sm(f"cln_b{L}", m, 1), scale=sm(f"cln_g{L}", m, 1)), y))
                tmp.release(rs, y)
                gd = []
                for m in range(4):
                    s1, p1, t1 = win(1024 + 128 * m, rx)
                    ts, sg, tf = tmp.take()
                    g = A(lambda e, sg=sg, p1=p1: e.activation(sg[:, 0:ntk], p1[:, 0:ntk], ACT.Silu), t1, tf)
                    pairs.release(s1, g)
                    y = V(lambda e, m=m, sg=sg: e.tensor_tensor(sg[:, 0:ntk], sg[:, 0:ntk], C[:, m, :], ALU.mult), g, lnd[m])
                    s = split_into(Gh[:, m, :], Gl[:, m, :], sg[:, 0:ntk], y)
                    tmp.release(ts, s)
                    gd.append(s)
                merge(0, "w_proj_a", Gh, Gl, gd)
            P.barrier()

            for br in range(2):
                wa = br == 1
                with ExitStack() as ph:
                    nk = 2 if wa else 4
                    nv = 2 if wa else 8
                    Q = sb(f"Q{L}{br}", [128, 4, ntk], F32, ph)
                    inner = ExitStack()
                    K = sb(f"K{L}{br}", [128, nk, NT], F32, inner)
                    VV = sb(f"V{L}{br}", [128, 6, nv, 65], F32, inner)
                    BI = [sb(f"BI{L}{br}{i}", [128, 512], F32, inner) for i in range(2)]
                    rope = []
                    if wa:
                        RC = sb(f"RC{L}", [128, 1024], F32, inner)
                        MK = sb(f"MK{L}", [128, 384], F32, inner)
                        rope = [P.dma("sync", "rc", RC[:, :], t["rope"][:, :], P.now()),
                                P.dma("sync", "mk", MK[:, :], t["wmask"][:, :], P.now())]
                    vone = G(lambda e, VV=VV: e.memset(VV[:, :, :, 64:65], 1.0), P.now())
                    cq, ck, cv, cg = (3584, 4096, 4224, 4352) if wa else (1536, 2048, 2560, 3072)
                    kvdone = [vone]
                    qdone = []

                    def normed(col, ranges, n, gain, dst, roped, pre):
                        s1, p1, t1 = win(col, ranges)
                        ts, q0, tf = tmp.take()
                        c0 = V(lambda e: e.tensor_copy(q0[:, 0:n], p1[:, 0:n]), t1, tf)
                        us, sq, uf = tmp.take()
                        a = A(lambda e: e.activation(sq[:, 0:n], q0[:, 0:n], ACT.Square), c0, uf)
                        pairs.release(s1, c0)
                        s2, p2, pf = pairs.take()
                        for a0, m, c in ranges:
                            tok = MM(lambda e, a0=a0, m=m, c=c: e.matmul(p2[:, c:c + m], bones, sq[:, a0:a0 + m], start=True, stop=True), a, pf)
                        tmp.release(us, tok)
                        us, sq, r, l = rsqrt(p2, n, 1.0 / 64, tok)
                        pairs.release(s2, l)
                        if not roped and len(dst) == 1:
                            y = V(lambda e: e.scalar_tensor_tensor(dst[0][1], q0[:, 0:n], gain, sq[:, 0:n], ALU.mult, ALU.mult), r, c0, pre)
                            tmp.release(us, y)
                            tmp.release(ts, y)
                            return [y]
                        y = V(lambda e: e.scalar_tensor_tensor(q0[:, 0:n], q0[:, 0:n], gain, sq[:, 0:n], ALU.mult, ALU.mult), r, c0)
                        s3, p3, pf = pairs.take()
                        tok = MM(lambda e: e.matmul(p3[:, 0:S], rmat, q0[:, 0:S], start=True, stop=True), y, pf)
                        b = V(lambda e: e.tensor_tensor(sq[:, 0:S], p3[:, 0:S], RC[:, S:2 * S], ALU.mult), tok, y, rope)
                        pairs.release(s3, b)
                        c1 = V(lambda e: e.tensor_tensor(q0[:, 0:S], q0[:, 0:S], RC[:, 0:S], ALU.mult), tok, rope)
                        outs = []
                        for (pa, pb), d in dst:
                            outs.append(V(lambda e, pa=pa, pb=pb, d=d: e.tensor_tensor(d[:, 0:S], q0[pa:pb, 0:S], sq[pa:pb, 0:S], ALU.add), b, c1, pre))
                            if n > S:
                                outs.append(A(lambda e, pa=pa, pb=pb, d=d: e.activation(d[:, S:n], q0[pa:pb, S:n], ACT.Copy), c1, pre))
                        tmp.release(us, outs)
                        tmp.release(ts, outs)
                        return outs

                    QG = sb(f"QG{L}{br}", [128, 1], F32, inner)
                    qg = V(lambda e: e.tensor_scalar(QG[:, :], sm(f"wa_q{L}" if wa else f"na_q{L}"), 0.125, None, ALU.mult))
                    for m in range(4):
                        qdone.append(normed(cq + 128 * m, rx, ntk, QG[:, 0:1], [((0, 128), Q[:, m, :])], wa, qg))
                    if wa:
                        dst = [((64 * g, 64 * g + 64), K[64 * hf:64 * hf + 64, g, :]) for g in range(2) for hf in range(2)]
                        kvdone.append(normed(ck, R768, NT, sm(f"wa_k{L}"), dst, True, None))
                    else:
                        for m in range(4):
                            kvdone.append(normed(ck + 128 * m, R768, NT, sm(f"na_k{L}"), [((0, 128), K[:, m, :])], False, None))
                    for m in range(1 if wa else 4):
                        s1, p1, t1 = win(cv + 128 * m, R768)
                        ts, vf, tf = tmp.take()
                        a = A(lambda e, vf=vf, p1=p1: e.activation(vf[:, :], p1[:, 0:NT], ACT.Copy), t1, tf)
                        pairs.release(s1, a)
                        s2, p2, pf = pairs.take()
                        for i in range(6):
                            tok = MM(lambda e, i=i, vf=vf, p2=p2: e.transpose(p2[:, 128 * i:128 * i + 128], vf[:, 128 * i:128 * i + 128], ident), a, pf, inc=(i == 5))
                        tmp.release(ts, tok)
                        y = V(lambda e, m=m, p2=p2: e.tensor_copy(VV[:, :, 2 * m:2 * m + 2, 0:64], p2[:, 0:768].rearrange("p (i h d) -> p i h d", i=6, h=2)), tok)
                        pairs.release(s2, y)
                        kvdone.append(y)

                    steps = []
                    bring = Ring(BI)
                    oring = Ring(tmps[4:6])
                    for i in range(2):
                        oring.free[i] = tmp.free[4 + i]
                    for qt in range(6 if L == 0 else 4):
                        isx = qt < 4
                        box = {}
                        for h in range(8):
                            hf = h % 2
                            pr = slice(64 * hf, 64 * hf + 64)
                            kt = h // 4 if wa else h // 2
                            vh = h // 4 if wa else h
                            if not isx:
                                lo_t, nw = 0, 0
                            elif wa:
                                lo_t = max(qt - 1, 0)
                                nw = 128 * (min(qt + 2, 4) - lo_t)
                            else:
                                lo_t, nw = 0, 512
                            ks = [(K[pr, kt, 128 * lo_t:128 * lo_t + nw], 512 - nw, nw)] if nw else []
                            ks.append((K[pr, kt, 512:768], 512, 256))
                            vs = [VV[:, lo_t + i, vh, :] for i in range(nw // 128)] + [VV[:, 4 + i, vh, :] for i in range(2)]

                            def bias(ps, tok, h=h, qt=qt, nw=nw, lo_t=lo_t):
                                if wa:
                                    o = 128 * (lo_t - (qt - 1))
                                    return V(lambda e: e.tensor_tensor(ps[:, 512 - nw:512], ps[:, 512 - nw:512], MK[:, o:o + nw], ALU.add), tok, rope)
                                bs, bt, bf = bring.take()
                                d = P.dma("sync", f"bi{bs}", bt[:, :], t[f"rpb{L}"][h, :, 64 * (7 - 2 * qt):64 * (7 - 2 * qt) + 512], bf)
                                y = V(lambda e: e.tensor_tensor(ps[:, 0:512], ps[:, 0:512], bt[:, :], ALU.add), tok, d)
                                bring.release(bs, y)
                                return y

                            def fin(o, r, d, h=h, box=box):
                                if h == 0:
                                    box["slot"], box["o"], box["free"] = oring.take()
                                ot = box["o"]
                                y = V(lambda e: e.tensor_scalar(ot[:, 64 * h:64 * h + 64], o, r, None, ALU.mult), d, box["free"])
                                box["done"] = y
                                return y

                            def post(tring, slot, qt=qt, box=box, Q=Q):
                                ps, free = tring.items[slot], tring.free[slot]
                                for i in range(4):
                                    tok = MM(lambda e, i=i: e.transpose(ps[:, 128 * i:128 * i + 128], box["o"][:, 128 * i:128 * i + 128], ident), free, box["done"], inc=(i == 3))
                                oring.release(box["slot"], tok)
                                y = V(lambda e: e.tensor_copy(Q[:, :, 128 * qt:128 * qt + 128], ps[:, 0:512].rearrange("p (m n) -> p m n", m=4)), tok)
                                tring.release(slot, y)

                            steps.append(dict(q=Q[pr, h // 2, 128 * qt:128 * qt + 128], ks=ks, a=512 - nw, b=768,
                                              bias=bias if isx else None, sink=sm(f"sink{L}", h, 1) if wa else None,
                                              vs=vs, fin=fin, post=post if h == 7 else None, act=(h % 2 == 0),
                                              wait=[qdone, kvdone]))
                    attention(steps)
                    for i in range(2):
                        tmp.free[4 + i] = oring.free[i]
                    inner.close()
                    P.barrier()
                    Gh = sb(f"Gh{L}{br}", [128, 4, ntk], F32R, ph)
                    Gl = sb(f"Gl{L}{br}", [128, 4, ntk], F32R, ph)
                    gd = []
                    for m in range(4):
                        s1, p1, t1 = win(cg + 128 * m, rx)
                        ts, sg, tf = tmp.take()
                        g = A(lambda e, sg=sg, p1=p1: e.activation(sg[:, 0:ntk], p1[:, 0:ntk], ACT.Silu), t1, tf)
                        pairs.release(s1, g)
                        y = V(lambda e, m=m, sg=sg: e.tensor_tensor(sg[:, 0:ntk], sg[:, 0:ntk], Q[:, m, :], ALU.mult), g)
                        s = split_into(Gh[:, m, :], Gl[:, m, :], sg[:, 0:ntk], y)
                        tmp.release(ts, s)
                        gd.append(s)
                    merge(1 + br, "w_proj_c" if wa else "w_proj_b", Gh, Gl, gd)
                P.barrier()

            yd = [split_into(Hh[:, k, 0:ntk], Hl[:, k, 0:ntk], Y[:, k, :], ydone[k]) for k in range(8)]
            x_done = []
            for m in range(8):
                s1, p1, t1 = linear([((f"w_o{L}", m, 0, 1024), list(range(8)))], lambda k: (Hh[:, k, :], Hl[:, k, :]), rx, yd)
                ys = [V(lambda e, m=m, q=q, a0=a0, n=n, p1=p1: e.scalar_tensor_tensor(xa(m, a0, n), p1[:, a0:a0 + n], MOD[:, 16 + m, q:q + 1], xa(m, a0, n), ALU.mult, ALU.add), t1)
                      for q, (a0, n, c) in enumerate(rx)]
                pairs.release(s1, ys)
                x_done.append(ys)
            lay.close()
            P.barrier()

        both.close()

        def plain_rms(name, hh, hl, waits):
            return rms(S, R512, waits, hh, hl, lambda k, q: sm(name, k, 1), lambda k, q: None)

        def add_out(name, nkt, parts_of, gh, gl, gdone):
            res = []
            for m in range(8):
                s1, p1, t1 = linear(parts_of(m), lambda k: (gh[:, k, :], gl[:, k, :]), R512, gdone)
                y = V(lambda e, m=m, p1=p1: e.tensor_tensor(X[:, m, 0:S], X[:, m, 0:S], p1[:, 0:S], ALU.add), t1)
                pairs.release(s1, y)
                res.append(y)
            return res

        def ffn(idx, x_done):
            with ExitStack() as ph:
                Gh = sb(f"FGh{idx}", [128, 24, S], F32R, ph)
                Gl = sb(f"FGl{idx}", [128, 24, S], F32R, ph)
                gd = []
                with ExitStack() as p2_:
                    Hh = sb(f"FHh{idx}", [128, 8, S], F32R, p2_)
                    Hl = sb(f"FHl{idx}", [128, 8, S], F32R, p2_)
                    hd = plain_rms(f"ffn_norm{idx}", Hh, Hl, x_done)
                    cw, cb = SM_AT[f"ffn_cw{idx}"][0], SM_AT[f"ffn_cb{idx}"][0]
                    for m in range(24):
                        s1, p1, t1 = linear([((f"ffn_in{idx}", m, 0, 1024), list(range(8)))], lambda k: (Hh[:, k, :], Hl[:, k, :]), R512, hd)
                        ts, pa, tf = tmp.take()
                        z = V(lambda e, pa=pa: e.memset(pa[:, 0:2], 0.0), tf)
                        a = A(lambda e, pa=pa, p1=p1: e.activation(pa[:, 2:2 + S], p1[:, 0:S], ACT.Copy), t1, tf)
                        pairs.release(s1, a)
                        us, u, uf = tmp.take()
                        y = V(lambda e, m=m, pa=pa, u=u: e.tensor_scalar(u[:, 0:S], pa[:, 0:S], smc(cw + 3 * m, cw + 3 * m + 1), smc(cb + m, cb + m + 1), ALU.mult, ALU.add), a, z, uf)
                        for k in (1, 2):
                            y = V(lambda e, m=m, k=k, pa=pa, u=u: e.scalar_tensor_tensor(u[:, 0:S], pa[:, k:k + S], smc(cw + 3 * m + k, cw + 3 * m + k + 1), u[:, 0:S], ALU.mult, ALU.add), y)
                        tmp.release(ts, y)
                        g = A(lambda e, u=u: e.activation(u[:, 0:S], u[:, 0:S], ACT.Gelu_apprx_tanh), y)
                        s2, p2, t2 = linear([((f"ffn_in{idx}", 24 + m, 0, 1024), list(range(8)))], lambda k: (Hh[:, k, :], Hl[:, k, :]), R512, hd)
                        y = V(lambda e, u=u, p2=p2: e.tensor_tensor(u[:, 0:S], u[:, 0:S], p2[:, 0:S], ALU.mult), g, t2)
                        pairs.release(s2, y)
                        s = split_into(Gh[:, m, :], Gl[:, m, :], u[:, 0:S], y)
                        tmp.release(us, s)
                        gd.append(s)
                res = add_out("ffn_out", 24, lambda m: [((f"ffn_out{idx}", m, 1024 * c, 1024), list(range(8 * c, 8 * c + 8))) for c in range(3)], Gh, Gl, gd)
            P.barrier()
            return res

        with ExitStack() as ph:
            YB = sb("YB", [128, 10, S], F32, ph)
            XC = sb("XC", [128, 10, S], F32, ph)
            RG = sb("RG", [128, 10, S], F32, ph)
            IG = sb("IG", [128, 10, S], F32, ph)
            C8 = sb("C8", [128, 8, 10], F32, ph)
            ap_ = sm("a_param")
            v = V(lambda e: e.scalar_tensor_tensor(C8[:, 0, :], ap_, -1.0, ap_, ALU.mult, ALU.max), P.now())
            a = A(lambda e: e.activation(C8[:, 1, :], C8[:, 0, :], ACT.Exp, scale=-1.0), v)
            v = V(lambda e: e.tensor_scalar(C8[:, 2, :], C8[:, 1, :], 2.0, None, ALU.add), a)
            v = V(lambda e: e.reciprocal(C8[:, 3, :], C8[:, 2, :]), v)
            v = V(lambda e: e.tensor_tensor(C8[:, 2, :], C8[:, 1, :], C8[:, 3, :], ALU.mult), v)
            v = V(lambda e: e.tensor_tensor(C8[:, 3, :], C8[:, 2, :], C8[:, 2, :], ALU.mult), v)
            v = V(lambda e: e.tensor_scalar(C8[:, 4, :], C8[:, 3, :], 1.0 / 19, 1.0 / 17, ALU.mult, ALU.add), v)
            for n in (15, 13, 11, 9, 7, 5, 3, 1):
                v = V(lambda e: e.tensor_tensor(C8[:, 4, :], C8[:, 4, :], C8[:, 3, :], ALU.mult), v)
                v = V(lambda e, n=n: e.tensor_scalar(C8[:, 4, :], C8[:, 4, :], 1.0 / n, None, ALU.add), v)
            v = V(lambda e: e.scalar_tensor_tensor(C8[:, 4, :], C8[:, 4, :], 2.0, C8[:, 2, :], ALU.mult, ALU.mult), v)
            v = V(lambda e: e.tensor_scalar(C8[:, 5, :], ap_, -1.0, 0.0, ALU.mult, ALU.max), v)
            v = V(lambda e: e.tensor_tensor(C8[:, 5, :], C8[:, 5, :], C8[:, 4, :], ALU.add), v)
            c8 = V(lambda e: e.tensor_scalar(C8[:, 6, :], C8[:, 5, :], -8.0, None, ALU.mult), v)
            with ExitStack() as p2_:
                Hh = sb("LHh", [128, 8, S], F32R, p2_)
                Hl = sb("LHl", [128, 8, S], F32R, p2_)
                XS = [sb("XS0", [128, 2, S], F32R, p2_)]
                xsr = Ring(XS)
                hd = plain_rms("lru_norm", Hh, Hl, x_done)

                def lru_in(m):
                    return linear([(("lru_in", m, 0, 1024), list(range(8)))], lambda k: (Hh[:, k, :], Hl[:, k, :]), R512, hd)

                yb = []
                for m in range(10):
                    s1, p1, t1 = lru_in(m)
                    a = A(lambda e, m=m, p1=p1: e.activation(YB[:, m, :], p1[:, 0:S], ACT.Gelu_apprx_tanh), t1)
                    pairs.release(s1, a)
                    yb.append(a)
                cw = SM_AT["lru_conv_w"][0]
                rg = []
                for m in range(10):
                    s1, p1, t1 = lru_in(10 + m)
                    ts, pa, tf = tmp.take()
                    z = V(lambda e, pa=pa: e.memset(pa[:, 0:3], 0.0), tf)
                    a = A(lambda e, pa=pa, p1=p1: e.activation(pa[:, 3:3 + S], p1[:, 0:S], ACT.Copy), t1, tf)
                    pairs.release(s1, a)
                    y = V(lambda e, m=m, pa=pa: e.tensor_scalar(XC[:, m, :], pa[:, 0:S], smc(cw + 4 * m, cw + 4 * m + 1), sm("lru_conv_b", m, 1), ALU.mult, ALU.add), a, z)
                    for k in (1, 2, 3):
                        y = V(lambda e, m=m, k=k, pa=pa: e.scalar_tensor_tensor(XC[:, m, :], pa[:, k:k + S], smc(cw + 4 * m + k, cw + 4 * m + k + 1), XC[:, m, :], ALU.mult, ALU.add), y)
                    tmp.release(ts, y)
                    xslot, xs, xf = xsr.take()
                    s = split_into(xs[:, 0, :], xs[:, 1, :], XC[:, m, :], y, xf)
                    (hi, lo), ready, j = chunk("gate_w", m, 0, 256)
                    pslot, pp, pf = pairs.take()
                    for g in range(2):
                        for q, (w, xi) in enumerate(((hi, 0), (hi, 1), (lo, 0))):
                            tok = MM(lambda e, g=g, q=q, w=w, xi=xi, pp=pp, xs=xs: e.matmul(pp[:, 512 * g:512 * g + 512], w[:, 128 * g:128 * g + 128], xs[:, xi, :], start=(q == 0), stop=(q == 2)),
                                     ready, s, pf, inc=(q == 2))
                    chunk_done(j, tok)
                    xsr.release(xslot, tok)
                    a1 = A(lambda e, m=m, pp=pp: e.activation(RG[:, m, :], pp[:, 0:S], ACT.Sigmoid, bias=sm("gate_b", m, 1)), tok)
                    a2 = A(lambda e, m=m, pp=pp: e.activation(IG[:, m, :], pp[:, 512:1024], ACT.Sigmoid, bias=sm("gate_b", 10 + m, 1)), tok)
                    pairs.release(pslot, a1, a2)
                    rg.append((a1, a2, y))
            P.barrier()
            with ExitStack() as p3_:
                Gh = sb("LGh", [128, 10, S], F32R, p3_)
                Gl = sb("LGl", [128, 10, S], F32R, p3_)
                us, ths = [], []
                for m in range(10):
                    i1 = V(lambda e, m=m: e.tensor_tensor(IG[:, m, :], IG[:, m, :], XC[:, m, :], ALU.mult), rg[m])
                    u = V(lambda e, m=m: e.tensor_scalar(RG[:, m, :], RG[:, m, :], C8[:, 6, m:m + 1], None, ALU.mult), rg[m], c8)
                    th = A(lambda e, m=m: e.activation(XC[:, m, :], RG[:, m, :], ACT.Tanh, scale=-1.0), u, i1)
                    ex = A(lambda e, m=m: e.activation(RG[:, m, :], RG[:, m, :], ACT.Exp), th)
                    us.append(ex)
                    ths.append((th, i1, ex))
                ys = []
                for m in range(10):
                    ts, d, tf = tmp.take()
                    y = V(lambda e, m=m, d=d: e.tensor_tensor(d[:, 0:S], RG[:, m, :], RG[:, m, :], ALU.mult), ths[m], tf)
                    y = V(lambda e, m=m, d=d: e.scalar_tensor_tensor(XC[:, m, :], d[:, 0:S], 1.0, XC[:, m, :], ALU.add, ALU.mult), y)
                    tmp.release(ts, y)
                    ys.append(A(lambda e, m=m: e.activation(XC[:, m, :], XC[:, m, :], ACT.Sqrt), y))
                gd = []
                for m in range(10):
                    y = V(lambda e, m=m: e.tensor_tensor(IG[:, m, :], IG[:, m, :], XC[:, m, :], ALU.mult), ys[m])
                    y = V(lambda e, m=m: e.tensor_tensor_scan(IG[:, m, :], RG[:, m, :], IG[:, m, :], 0.0, ALU.mult, ALU.add), y, us[m])
                    y = V(lambda e, m=m: e.tensor_tensor(IG[:, m, :], IG[:, m, :], YB[:, m, :], ALU.mult), y, yb[m])
                    gd.append(split_into(Gh[:, m, :], Gl[:, m, :], IG[:, m, :], y))
                x_done = add_out("lru_out", 10, lambda m: [(("lru_out", m, 640 * c, 640), list(range(5 * c, 5 * c + 5))) for c in range(2)], Gh, Gl, gd)
        P.barrier()

        x_done = ffn(0, x_done)

        with ExitStack() as ph:
            gd = []
            inner = ExitStack()
            with inner:
                Q = sb("NQ", [128, 8, S], F32, inner)
                KD = [sb(f"KD{b}", [128, 4, S], F32, inner) for b in range(2)]
                VN = [sb(f"VN{b}", [128, 4, 4, 65], F32, inner) for b in range(2)]
                GT = sb("GT", [128, 4, 48], F32, inner)
                KC = sb("KC", [128, 128], F32, inner)
                VB = sb("VB", [128, 4, 256], F32, inner)
                TB = sb("TB", [128, 512], F32, inner)
                RV = sb("RV", [128, 4], F32, inner)
                now = P.now()
                tb = [P.dma("sync", "tb", TB[:, :], t["ntab"][:, :], now), P.dma("sync", "rv", RV[:, :], t["rowok"][:, :], now)]
                von = [G(lambda e, b=b: e.memset(VN[b][:, :, :, 64:65], 1.0), now) for b in range(2)]
                vz = G(lambda e: e.memset(VB[:, :, :], 0.0), now)
                qd, kd, vd = [], [[], []], [[von[0]], [von[1]]]
                with ExitStack() as p2_:
                    Hh = sb("NHh", [128, 8, S], F32R, p2_)
                    Hl = sb("NHl", [128, 8, S], F32R, p2_)
                    hd = plain_rms("nsa_norm", Hh, Hl, x_done)

                    def nin(m):
                        return linear([(("nsa_in", m, 0, 1024), list(range(8)))], lambda k: (Hh[:, k, :], Hl[:, k, :]), R512, hd)

                    for m in range(8):
                        s1, p1, t1 = nin(m)
                        a = A(lambda e, m=m, p1=p1: e.activation(Q[:, m, :], p1[:, 0:S], ACT.Copy, scale=0.125), t1)
                        pairs.release(s1, a)
                        qd.append(a)
                    s1, p1, t1 = nin(20)
                    ts, gs, tf = tmp.take()
                    a = A(lambda e: e.activation(gs[:, 0:S], p1[:, 0:S], ACT.Sigmoid), t1, tf)
                    pairs.release(s1, a)
                    s2, p2, pf = pairs.take()
                    for i in range(4):
                        tok = MM(lambda e, i=i: e.transpose(p2[:, 128 * i:128 * i + 128], gs[:, 128 * i:128 * i + 128], ident), a, pf, inc=(i == 3))
                    tmp.release(ts, tok)
                    gtd = V(lambda e: e.tensor_copy(GT[:, :, :], p2[:, 0:512].rearrange("p (i n) -> p i n", i=4)[:, :, 0:48]), tok)
                    pairs.release(s2, gtd)
                    for b in range(2):
                        c0 = 8 + 4 * (b + 1)
                        for m in range(2):
                            s1, p1, t1 = nin(c0 + m)
                            ys = []
                            for g in range(2):
                                for hf in range(2):
                                    f = (A if m else V)
                                    def cp(e, b=b, m=m, g=g, hf=hf, p1=p1):
                                        o, i = KD[b][64 * hf:64 * hf + 64, 2 * m + g, :], p1[64 * g:64 * g + 64, 0:S]
                                        return e.activation(o, i, ACT.Copy) if m else e.tensor_copy(o, i)
                                    ys.append(f(cp, t1))
                            pairs.release(s1, ys)
                            kd[b] += ys
                        for m in range(2):
                            s1, p1, t1 = nin(c0 + 2 + m)
                            ts, vf, tf = tmp.take()
                            a = A(lambda e, vf=vf, p1=p1: e.activation(vf[:, 0:S], p1[:, 0:S], ACT.Copy), t1, tf)
                            pairs.release(s1, a)
                            s2, p2, pf = pairs.take()
                            for i in range(4):
                                tok = MM(lambda e, i=i, vf=vf, p2=p2: e.transpose(p2[:, 128 * i:128 * i + 128], vf[:, 128 * i:128 * i + 128], ident), a, pf, inc=(i == 3))
                            tmp.release(ts, tok)
                            y = V(lambda e, m=m, b=b, p2=p2: e.tensor_copy(VN[b][:, :, 2 * m:2 * m + 2, 0:64], p2[:, 0:512].rearrange("p (i h d) -> p i h d", i=4, h=2)), tok)
                            pairs.release(s2, y)
                            vd[b].append(y)
                    CF = sb("CF", [128, 4, 544], F32, p2_)
                    RH = sb("RH", [128, 16, 128], F32R, p2_)
                    RL = sb("RL", [128, 16, 128], F32R, p2_)
                    HID = sb("HID", [128, 2, 128], F32, p2_)
                    w2o = SM_AT["cmp_w2"][0]
                    cfz = G(lambda e: e.memset(CF[:, :, 504:544], 0.0), P.now())
                    prev = []
                    cmpd = []
                    for kv in range(2):
                        cf = []
                        for m in range(2):
                            s1, p1, t1 = nin(8 + 2 * kv + m)
                            ys = []
                            for g in range(2):
                                ys.append(V(lambda e, m=m, g=g, p1=p1: e.tensor_copy(CF[0:64, 2 * m + g, 0:S], p1[64 * g:64 * g + 64, 0:S]), t1, cfz, prev))
                                ys.append(V(lambda e, m=m, g=g, p1=p1: e.tensor_copy(CF[64:128, 2 * m + g, 0:S - 1], p1[64 * g:64 * g + 64, 1:S]), t1, cfz, prev))
                            pairs.release(s1, ys)
                            cf += ys
                        po = SM_AT["cmp_pos"][0] + 16 * kv
                        rd = []
                        for k in range(16):
                            ts, rr, tf = tmp.take()
                            src = CF[:, :, 2 * k:2 * k + 512].rearrange("p g (j s) -> p g j s", s=16)[:, :, :, 0]
                            y = V(lambda e, k=k, rr=rr, src=src, po=po: e.tensor_scalar(rr[:, 0:128].rearrange("p (g j) -> p g j", g=4), src, smc(po + k, po + k + 1), None, ALU.add), cf, tf)
                            s = split_into(RH[:, k, :], RL[:, k, :], rr[:, 0:128], y, prev)
                            tmp.release(ts, s)
                            rd.append(s)
                        hd2 = []
                        for m in range(2):
                            s1, p1, t1 = linear([(("cmp_w1", 2 * kv + m, 1024 * c, 1024), list(range(8 * c, 8 * c + 8))) for c in range(2)],
                                                lambda k: (RH[:, k, :], RL[:, k, :]), [(0, 128, 0)], rd)
                            a = A(lambda e, m=m, kv=kv, p1=p1: e.activation(HID[:, m, :], p1[:, 0:128], ACT.Gelu_apprx_tanh, bias=sm("cmp_b1", 2 * kv + m, 1)), t1, prev)
                            pairs.release(s1, a)
                            hd2.append(a)
                        s1, p1, pf = pairs.take()
                        if kv == 0:
                            for hf in range(2):
                                for k in range(2):
                                    tok = MM(lambda e, k=k, hf=hf, p1=p1: e.matmul(p1[64 * hf:64 * hf + 64, 0:128], smc(w2o + 64 * k, w2o + 64 * k + 64), HID[:, k, :], start=(k == 0), stop=(k == 1)), hd2, pf)
                            y = V(lambda e, p1=p1: e.tensor_copy(KC[:, :], p1[:, 0:128]), tok)
                            cmpd.append(y)
                            prev = [y]
                        else:
                            for g in range(4):
                                for k in range(2):
                                    hsrc = HID[:, k, 32 * g:32 * g + 32]
                                    for q in range(4):
                                        tok = MM(lambda e, k=k, g=g, q=q, hsrc=hsrc, p1=p1: e.matmul(p1[32 * q:32 * q + 32, 64 * g:64 * g + 64], hsrc, smc(w2o + 128 + 64 * k, w2o + 192 + 64 * k), start=(k == 0), stop=(k == 1), skip_group_check=True), hd2, pf)
                            y = []
                            for q in range(4):
                                y.append(V(lambda e, q=q, p1=p1: e.tensor_copy(VB[32 * q:32 * q + 32, :, 64 * q:64 * q + 64], p1[32 * q:32 * q + 32, 0:256].rearrange("p (g d) -> p g d", g=4)), tok, vz))
                            cmpd += y
                        pairs.release(s1, y)
                P.barrier()
                Gh = sb("NGh", [128, 8, S], F32R, inner)
                Gl = sb("NGl", [128, 8, S], F32R, inner)
                OT = [sb(f"OT{i}", [128, 1024], F32, inner) for i in range(2)]
                CB = [sb(f"CB{i}", [128, 512], F32, inner) for i in range(2)]
                otr, cbr = Ring(OT), Ring(CB)
                slopes = [float(np.float32(2.0 ** (-8.0 * (h + 1) / 16))) for h in range(16)]
                for qt in range(4):
                    oslot, ot, of = otr.take()
                    cslot, cb, cf = cbr.take()
                    d = P.dma("sync", f"cb{cslot}", cb[:, :], t["ctab"][qt, :, :], cf)
                    s1, p1, pf = pairs.take()
                    for h in range(16):
                        pr = slice(64 * (h % 2), 64 * (h % 2) + 64)
                        tok = MM(lambda e, h=h, pr=pr, p1=p1, qt=qt: e.matmul(p1[:, 512 * (h % 2) + 32 * (h // 2):512 * (h % 2) + 32 * (h // 2) + 32], Q[pr, h // 2, 128 * qt:128 * qt + 128], KC[pr, 32 * (h // 4):32 * (h // 4) + 32], start=True, stop=True),
                                 qd, cmpd, pf, inc=(h == 15))
                    ts, pc, tf = tmp.take()
                    ss, sv, sf = tmp.take()
                    y = V(lambda e, pc=pc, p1=p1, cb=cb: e.tensor_tensor(
                        pc[:, 0:512].rearrange("p (t b j) -> p b t j", t=8, b=2),
                        p1.rearrange("p (b t j) -> p b t j", b=2, j=32)[:, :, 0:8, :],
                        cb[:, :].rearrange("p (t b j) -> p b t j", t=8, b=2), ALU.add), tok, d, tf)
                    cbr.release(cslot, y)
                    pairs.release(s1, y)
                    pc3 = pc[:, 0:512].rearrange("p (h j) -> p h j", h=16)
                    y = V(lambda e, sv=sv, pc3=pc3: e.tensor_reduce(sv[:, 0:16], pc3, AX.X, ALU.max), y, sf)
                    y = V(lambda e, sv=sv, pc3=pc3: e.tensor_tensor(pc3, pc3, sv[:, 0:16].unsqueeze(2).broadcast_to([128, 16, 32]), ALU.subtract), y)
                    a = A(lambda e, pc=pc: e.activation(pc[:, 0:512], pc[:, 0:512], ACT.Exp), y)
                    y = V(lambda e, sv=sv, pc3=pc3: e.tensor_reduce(sv[:, 16:32], pc3, AX.X, ALU.add), a)
                    y = V(lambda e, sv=sv: e.reciprocal(sv[:, 32:48], sv[:, 16:32]), y)
                    y = V(lambda e, sv=sv, qt=qt: e.scalar_tensor_tensor(sv[:, 48:64], sv[:, 32:48], RV[:, qt:qt + 1], GT[:, qt, 0:16], ALU.mult, ALU.mult), y, gtd, tb)
                    s2, p2, pf = pairs.take()
                    for i in range(4):
                        tok = MM(lambda e, i=i, pc=pc, p2=p2: e.transpose(p2[:, 128 * i:128 * i + 128], pc[:, 128 * i:128 * i + 128], ident), a, pf, inc=(i == 3))
                    us, pt, uf = tmp.take()
                    a = A(lambda e, pt=pt, p2=p2: e.activation(pt[:, 0:512], p2[:, 0:512], ACT.Copy), tok, uf)
                    pairs.release(s2, a)
                    tmp.release(ts, a)
                    s3, p3, pf = pairs.take()
                    for g in range(4):
                        tok = MM(lambda e, g=g, pt=pt, p3=p3: e.matmul(p3[:, 256 * g:256 * g + 256], pt[:, 128 * g:128 * g + 128], VB[:, g, :], start=True, stop=True), a, pf, inc=(g == 3))
                    tmp.release(us, tok)
                    od = V(lambda e, ot=ot, p3=p3, sv=sv: e.tensor_tensor(ot[:, :].rearrange("p (h d) -> p h d", h=16), p3.rearrange("p (h d) -> p h d", h=16), sv[:, 48:64].unsqueeze(2).broadcast_to([128, 16, 64]), ALU.mult), tok, y, of)
                    pairs.release(s3, od)
                    tmp.release(ss, od)
                    steps = []
                    nw = 128 * (qt + 1)
                    last = {"t": od}
                    for h in range(16):
                        pr = slice(64 * (h % 2), 64 * (h % 2) + 64)
                        g = h // 4
                        for b in range(2):
                            def bias(ps, tok, h=h, nw=nw):
                                return V(lambda e: e.scalar_tensor_tensor(ps[:, 512 - nw:512], TB[:, 512 - nw:512], -slopes[h], ps[:, 512 - nw:512], ALU.mult, ALU.add), tok, tb)

                            def fin(o, r, d, h=h, b=b, qt=qt, ot=ot, last=last):
                                y = V(lambda e: e.tensor_tensor(r, r, GT[:, qt, 16 * (b + 1) + h:16 * (b + 1) + h + 1], ALU.mult), d)
                                y = V(lambda e: e.scalar_tensor_tensor(ot[:, 64 * h:64 * h + 64], o, r, ot[:, 64 * h:64 * h + 64], ALU.mult, ALU.add), y, last["t"])
                                last["t"] = y
                                return y

                            steps.append(dict(q=Q[pr, h // 2, 128 * qt:128 * qt + 128], ks=[(KD[b][pr, g, 0:nw], 512 - nw, nw)],
                                              a=512 - nw, b=512, bias=bias, sink=None, vs=[VN[b][:, i, g, :] for i in range(qt + 1)],
                                              fin=fin, post=None, act=True, wait=[qd, kd[b], vd[b]]))
                    attention(steps)
                    s1, p1, pf = pairs.take()
                    for i in range(8):
                        tok = MM(lambda e, i=i, ot=ot, p1=p1: e.transpose(p1[:, 128 * i:128 * i + 128], ot[:, 128 * i:128 * i + 128], ident), last["t"], pf, inc=(i == 7))
                    otr.release(oslot, tok)
                    p8 = p1.rearrange("p (m n) -> p m n", m=8)
                    hi, lo = Gh[:, :, 128 * qt:128 * qt + 128], Gl[:, :, 128 * qt:128 * qt + 128]
                    s = split_into(hi, lo, p8, tok)
                    pairs.release(s1, s)
                    gd.append(s)
                x_done = add_out("nsa_out", 8, lambda m: [(("nsa_out", m, 0, 1024), list(range(8)))], Gh, Gl, gd)
        P.barrier()

        x_done = ffn(1, x_done)

        slot, ps, free = pairs.take()
        for k in range(8):
            ts, sq, tf = tmp.take()
            a = A(lambda e, k=k, sq=sq: e.activation(sq[:, 0:S], X[:, k, 0:S], ACT.Square), x_done, tf)
            tok = MM(lambda e, k=k, sq=sq, ps=ps: e.matmul(ps[:, 0:S], ones, sq[:, 0:S], start=(k == 0), stop=(k == 7)), a, free)
            tmp.release(ts, tok)
        rs, ri, r, l = rsqrt(ps, S, 1.0 / 1024, tok)
        pairs.release(slot, l)
        fd = [V(lambda e, k=k: e.scalar_tensor_tensor(X[:, k, 0:S], X[:, k, 0:S], sm("final_g", k, 1), ri[:, 0:S], ALU.mult, ALU.mult), r) for k in range(8)]
        with ExitStack() as ph:
            OU = [sb(f"OU{i}", [128, 1024], F32, ph) for i in range(2)]
            our = Ring(OU)
            outs = []
            for i in range(4):
                slot, ps, free = pairs.take()
                for k in range(8):
                    tok = MM(lambda e, i=i, k=k, ps=ps: e.transpose(ps[:, 128 * k:128 * k + 128], X[:, k, 128 * i:128 * i + 128], ident), fd, free, inc=(k == 7))
                os_, ou, of = our.take()
                y = V(lambda e, ou=ou, ps=ps: e.tensor_copy(ou[:, 0:512], ps[:, 0:512]), tok, of)
                z = A(lambda e, ou=ou, ps=ps: e.activation(ou[:, 512:1024], ps[:, 512:1024], ACT.Copy), tok, of)
                pairs.release(slot, y, z)
                d = P.dma("sync", f"ou{os_}", out[128 * i:128 * i + 128, :], ou[:, :], y, z)
                our.release(os_, d)
                outs.append(d)
        P.queue["sync"].append((flat(outs), None, None, 0))
        if order:
            P.emit(nc, sems)
    return log


DMA_SEMS = [f"w{i}" for i in range(NRAW)] + ["sm", "sm2", "co", "xt0", "xt1", "xt2", "rc", "mk", "bi0", "bi1", "tb", "rv", "cb0", "cb1", "ou0", "ou1"]


def program(nc, make, t, out):
    order = build(make(), t, out, [], {})
    with ExitStack() as ctx:
        sems = {name: ctx.enter_context(nc.semaphore("s_" + name)) for name in list(ENGINES) + DMA_SEMS}
        build(nc, t, out, order, sems)


def constants():
    co = np.zeros((128, 512), np.float32)
    co[:, 0:128] = np.eye(128)
    co[:, 128:256] = 1
    co[0:64, 256:320] = 1
    co[64:128, 320:384] = 1
    for m in range(128):
        if m % 32 < 16:
            co[m + 16, 384 + m] = -1
        else:
            co[m - 16, 384 + m] = 1
    inv = np.float32(10000.0) ** (-np.arange(16, dtype=np.float32) / np.float32(16))
    s = np.arange(S)
    rope = np.zeros((128, 1024), np.float32)
    for p in range(128):
        pos = (s // 64 if (p % 64) < 32 else s % 64).astype(np.float32)
        ang = pos * inv[p % 16]
        rope[p, 0:S] = np.cos(ang)
        rope[p, S:] = np.sin(ang)
    p = np.arange(128)[:, None]
    y = np.arange(384)[None, :]
    wmask = np.where(np.abs(y - 128 - p) <= 128, 0.0, NEG).astype(np.float32)
    y = np.arange(512)[None, :] - 384
    ntab = np.where(p >= y, p - y, FAR).astype(np.float32)
    sl = 2.0 ** (-8.0 * np.arange(1, 17) / 16)
    ctab = np.zeros((4, 128, 16, 32), np.float32)
    rowok = np.zeros((128, 4), np.float32)
    for qt in range(4):
        tt = 128 * qt + np.arange(128)
        j = np.arange(32)
        dist = tt[:, None] - (16 * j[None, :] + 15.5)
        ok = (16 * j[None, :] + 31 <= tt[:, None]) & (j[None, :] < 31)
        ctab[qt] = np.where(ok[:, None, :], -sl.astype(np.float32)[None, :, None] * dist.astype(np.float32)[:, None, :], NEG)
        rowok[:, qt] = ok.any(1)
    return {"co": co, "rope": rope, "wmask": wmask, "ntab": ntab, "ctab": ctab.reshape(4, 128, 512), "rowok": rowok}


def pack(w):
    k, n = w.shape
    if n % 128:
        w = np.concatenate([w, np.zeros((k, 128 - n % 128), w.dtype)], 1)
        n = w.shape[1]
    return np.ascontiguousarray(w.reshape(k // 128, 128, n // 128, 128).transpose(2, 1, 0, 3).reshape(n // 128, 128, k))


def layout(i):
    d = dict(constants())
    d["x"], d["ctx"] = i["x"][0], i["ctx"][0]
    for l in range(2):
        for n in ("w_ada", "w_in", "w_proj_a", "w_proj_b", "w_proj_c", "w_o"):
            d[f"{n}{l}"] = pack(i[n][l])
        pad = np.full((8, 15, 64, 64), NEG, np.float32)
        for j in range(64):
            c0 = min(max(j - 8, 0), 48)
            pad[:, :, j, c0:c0 + 16] = i["na_rpb"][l][:, :, c0 - j + 15:c0 - j + 31]
        b = np.zeros((8, 2, 64, 15, 64), np.float32)
        tab = pad.transpose(0, 2, 1, 3)
        b[:, 0] = tab
        b[:, 1, :, 1:] = tab[:, :, :14]
        d[f"rpb{l}"] = b.reshape(8, 128, 960)
        d[f"ffn_in{l}"] = pack(i["ffn_w_in_2"][l])
        d[f"ffn_out{l}"] = pack(i["ffn_w_out_2"][l])
    d["lru_in"] = pack(i["lru_w_in_2"][0])
    d["lru_out"] = pack(i["lru_w_out_2"][0])
    d["gate_w"] = i["lru_gate_w_2"][0].transpose(1, 2, 0, 3).reshape(10, 128, 256)
    d["nsa_in"] = pack(i["nsa_w_in_2"][0])
    d["nsa_out"] = pack(i["nsa_w_out_2"][0])
    d["cmp_w1"] = np.concatenate([pack(i["nsa_cmp_w1_2"][0, k]) for k in range(2)])
    sm = np.zeros((128, SM_N), np.float32)

    def put(name, a):
        o, w = SM_AT[name]
        sm[:, o:o + w] = a.reshape(a.shape[0], -1)

    def col(v):
        return v.reshape(-1, 128).T

    put("cc", np.stack([col(i["c"][0]), col(i["c_ctx"])], 2))
    for l in range(2):
        put(f"norm_g{l}", col(i["norm_g"][l]))
        put(f"b_ada{l}", col(i["b_ada"][l]))
        put(f"conv_w{l}", i["conv_w"][l].reshape(31, 4, 128).transpose(2, 1, 0))
        put(f"conv_b{l}", col(i["conv_b"][l]))
        put(f"cln_g{l}", col(i["cln_g"][l]))
        put(f"cln_b{l}", col(i["cln_b"][l]))
        for a, b in (("na_q", "na_q_norm"), ("na_k", "na_k_norm"), ("wa_q", "wa_q_norm"), ("wa_k", "wa_k_norm")):
            put(f"{a}{l}", np.tile(i[b][l], 2)[:, None])
        put(f"sink{l}", np.tile(i["wa_sink"][l][None], (128, 1)))
        put(f"ffn_norm{l}", col(i["ffn_norm_g_2"][l]))
        put(f"ffn_cw{l}", i["ffn_conv_w_2"][l].reshape(3, 24, 128).transpose(2, 1, 0))
        put(f"ffn_cb{l}", col(i["ffn_conv_b_2"][l]))
    put("lru_norm", col(i["lru_norm_g_2"][0]))
    put("lru_conv_w", i["lru_conv_w_2"][0].reshape(4, 10, 128).transpose(2, 1, 0))
    put("lru_conv_b", col(i["lru_conv_b_2"][0]))
    put("gate_b", i["lru_gate_b_2"][0].reshape(2, 10, 128).transpose(2, 0, 1))
    put("a_param", col(i["lru_a_param_2"][0]))
    put("nsa_norm", col(i["nsa_norm_g_2"][0]))
    put("cmp_pos", i["nsa_cmp_pos_2"][0].reshape(2, 16, 128).transpose(2, 0, 1))
    put("cmp_b1", i["nsa_cmp_b1_2"][0].reshape(2, 2, 128).transpose(2, 0, 1))
    put("cmp_w2", i["nsa_cmp_w2_2"][0].reshape(2, 2, 128, 64).transpose(2, 0, 1, 3))
    put("final_g", col(i["final_norm_g_2"]))
    d["sm"] = sm
    return d


def kernel(**inputs):
    import concourse.bacc as bacc
    from concourse.bass_utils import run_bass_kernel_spmd

    i = {k: np.asarray(v) for k, v in inputs.items()}
    d = layout(i)

    def make():
        return bacc.Bacc("TRN2", target_bir_lowering=False, num_devices=1)

    nc = make()
    arrays, t = {}, {}
    for name, a in d.items():
        a = np.ascontiguousarray(a, dtype=np.float32)
        arrays[f"in_{name}"] = a
        t[name] = nc.dram_tensor(f"in_{name}", a.shape, F32, kind="ExternalInput").ap()
    out = nc.dram_tensor("out_0", (S, 1024), F32, kind="ExternalOutput").ap()
    program(nc, make, t, out)
    r = run_bass_kernel_spmd(nc, [arrays], core_ids=[0])
    return r.results[0]["out_0"].reshape(1, S, 1024)
```

```python
import math
from contextlib import ExitStack

import numpy as np
import concourse.bass as bass
from concourse import mybir

F32 = mybir.dt.float32
F32R = mybir.dt.float32r
ALU = mybir.AluOpType
ACT = mybir.ActivationFunctionType
AX = mybir.AxisListType

S = 512
NCTX = 256
NT = S + NCTX
EPS = 1e-6
NEG = -1e30
FAR = 1e33
NRAW = 3
NSPL = 3
NMOD = 9
ENGINES = ("tensor", "vector", "scalar", "gpsimd", "sync")

SM_PARTS = [("cc", 16)]
for _l in range(2):
    SM_PARTS += [(f"norm_g{_l}", 8), (f"b_ada{_l}", 24), (f"conv_w{_l}", 124), (f"conv_b{_l}", 4),
                 (f"cln_g{_l}", 4), (f"cln_b{_l}", 4), (f"na_q{_l}", 1), (f"na_k{_l}", 1),
                 (f"wa_q{_l}", 1), (f"wa_k{_l}", 1), (f"sink{_l}", 8)]
SM_PARTS += [("lru_norm", 8), ("lru_conv_w", 40), ("lru_conv_b", 10), ("gate_b", 20), ("a_param", 10),
             ("nsa_norm", 8), ("cmp_pos", 32), ("cmp_b1", 4), ("cmp_w2", 256), ("ffn_norm0", 8),
             ("ffn_norm1", 8), ("ffn_cw0", 72), ("ffn_cw1", 72), ("ffn_cb0", 24), ("ffn_cb1", 24),
             ("final_g", 8)]
SM_AT = {}
_n = 0
for _k, _w in SM_PARTS:
    SM_AT[_k] = (_n, _w)
    _n += _w
SM_N = _n
SM_1 = SM_AT["lru_norm"][0]


class Call:

    def matmul(self, *a, **k): return lambda e: e.matmul(*a, **k)
    def transpose(self, *a, **k): return lambda e: e.transpose(*a, **k)
    def activation(self, *a, **k): return lambda e: e.activation(*a, **k)
    def tensor_copy(self, *a, **k): return lambda e: e.tensor_copy(*a, **k)
    def tensor_tensor(self, *a, **k): return lambda e: e.tensor_tensor(*a, **k)
    def tensor_scalar(self, *a, **k): return lambda e: e.tensor_scalar(*a, **k)
    def scalar_tensor_tensor(self, *a, **k): return lambda e: e.scalar_tensor_tensor(*a, **k)
    def tensor_tensor_scan(self, *a, **k): return lambda e: e.tensor_tensor_scan(*a, **k)
    def tensor_reduce(self, *a, **k): return lambda e: e.tensor_reduce(*a, **k)
    def reciprocal(self, *a, **k): return lambda e: e.reciprocal(*a, **k)
    def memset(self, *a, **k): return lambda e: e.memset(*a, **k)


CALL = Call()


class Program:

    def __init__(self):
        self.queue = {e: [] for e in ENGINES}
        self.count = {e: 0 for e in ENGINES}
        self.dma_count = {}

    def op(self, engine, fn, *waits, inc=True):
        self.queue[engine].append((flat(waits), fn(CALL), engine if inc else None, 1))
        if inc:
            self.count[engine] += 1
            return (engine, self.count[engine])
        return None

    def dma(self, engine, sem, dst, src, *waits):
        self.dma_count[sem] = self.dma_count.get(sem, 0) + 16
        self.queue[engine].append((flat(waits), lambda e: e.dma_start(dst, src), sem, 16))
        return (sem, self.dma_count[sem])

    def now(self):
        return [(e, c) for e, c in self.count.items() if c]

    def barrier(self):
        now = self.now()
        for e in ENGINES:
            self.queue[e].append((now, None, None, 0))
        return now

    def emit(self, nc, sems):
        with nc.Block() as block:
            for name in ENGINES:
                def body(e, name=name):
                    seen = {}
                    for waits, fn, sem, step in self.queue[name]:
                        for s, v in waits:
                            if seen.get(s, 0) < v:
                                e.wait_ge(sems[s], v)
                                seen[s] = v
                        if fn is not None:
                            ins = fn(e)
                            if sem is not None:
                                ins.then_inc(sems[sem], step)
                enter = {"tensor": block.tensor, "vector": block.vector, "scalar": block.scalar,
                                 "gpsimd": block.gpsimd, "sync": block.sync}[name]
                enter(body)


def flat(waits):
    best = {}
    stack = [waits]
    while stack:
        w = stack.pop()
        if w is None:
            continue
        if isinstance(w, tuple) and len(w) == 2 and isinstance(w[0], str):
            best[w[0]] = max(best.get(w[0], 0), w[1])
        else:
            stack.extend(w)
    return sorted(best.items())


class Ring:

    def __init__(self, items):
        self.items = items
        self.free = [[] for _ in items]
        self.idle = list(range(len(items)))

    def take(self):
        slot = self.idle.pop(0)
        return slot, self.items[slot], self.free[slot]

    def release(self, slot, *tokens):
        assert slot not in self.idle
        self.idle.append(slot)
        self.free[slot] = list(tokens)

    def lend(self, slots):
        assert all(i in self.idle for i in slots)
        ring = Ring([self.items[i] for i in slots])
        ring.free = [self.free[i] for i in slots]
        self.idle = [i for i in self.idle if i not in slots]
        return ring

    def give_back(self, ring, slots):
        assert len(ring.idle) == len(slots)
        for n, i in enumerate(slots):
            self.release(i, ring.free[n])


def pipeline(tasks):
    active = []
    for g in tasks:
        next(g)
        active = [a for a in active if next(a, "end") != "end"] + [g]
    while active:
        active = [a for a in active if next(a, "end") != "end"]


def build(nc, t, out, order, sems_out):
    P = Program()
    ctx = ExitStack()
    log = []

    def sb(name, shape, dt=F32, stack=ctx):
        return stack.enter_context(nc.sbuf_tensor(name, shape, dt))

    with ctx:
        X = sb("X", [128, 8, S])
        RAW = [sb(f"RAW{i}", [128, 1024]) for i in range(NRAW)]
        WH = [sb(f"WH{i}", [128, 1024], F32R) for i in range(NSPL)]
        WL = [sb(f"WL{i}", [128, 1024], F32R) for i in range(NSPL)]
        SM = sb("SM", [128, SM_N - SM_1])
        CO = sb("CO", [128, 512])
        MODS = [sb(f"MOD{i}", [128, 24, 2]) for i in range(2)]
        AB = sb("AB", [128, 8, 2])
        EPSC = sb("EPSC", [128, 1])
        STAT = sb("STAT", [128, 8, 8])
        PS = ctx.enter_context(nc.psum_tensor("PS", [128, 4, 1024], F32))
        sems = sems_out

        ident = CO[:, 0:128]
        ones = CO[:, 128:256]
        bones = CO[:, 256:384]
        rmat = CO[:, 384:512]

        def smc(a, b):
            return SMA[:, a:b] if a < SM_1 else SM[:, a - SM_1:b - SM_1]

        def sm(name, a=0, n=None):
            o, w = SM_AT[name]
            return smc(o + a, o + a + (w - a if n is None else n))

        def V(fn, *w): return P.op("vector", fn, *w)
        def A(fn, *w): return P.op("scalar", fn, *w)
        def G(fn, *w): return P.op("gpsimd", fn, *w)
        def MM(fn, *w, inc=True): return P.op("tensor", fn, *w, inc=inc)

        pairs = Ring([PS[:, i, :] for i in range(4)])
        stat = Ring([STAT[:, i, :] for i in range(8)])

        st = {"dma": 0, "split": 0, "spl": 0, "use": 0}
        raw_free = {}
        raw_ready = {}
        split_ready = {}
        spl_free = {}
        spl_slot = {}

        def pump_dma():
            while st["dma"] < len(order):
                j = st["dma"]
                if j >= NRAW and (j - NRAW) not in raw_free:
                    return
                name, idx, c0, n, _ = order[j]
                raw_ready[j] = P.dma("sync", f"w{j % NRAW}", RAW[j % NRAW][:, 0:n], t[name][idx, :, c0:c0 + n],
                                     raw_free.get(j - NRAW))
                st["dma"] += 1

        def split_next():
            j = st["split"]
            name, idx, c0, n, split = order[j]
            if split:
                k = st["spl"]
                slot = k % NSPL
                wait = spl_free.get(k - NSPL)
                src = RAW[j % NRAW][:, 0:n]
                hi, lo = WH[slot][:, 0:n], WL[slot][:, 0:n]
                a = A(lambda e: e.activation(hi, src, ACT.Copy), raw_ready[j], wait)
                b = (G if split == 2 else V)(lambda e: e.tensor_tensor(lo, src, hi.bitcast(F32), ALU.subtract), a)
                raw_free[j] = [a, b]
                split_ready[j] = b
                spl_slot[j] = (slot, k)
                st["spl"] += 1
                st["split"] += 1
                pump_dma()
            else:
                st["split"] += 1

        def chunk(name, idx, c0, n, split=True):
            log.append((name, idx, c0, n, split))
            j = st["use"]
            st["use"] += 1
            if not order:
                return (WH[0][:, 0:n], WL[0][:, 0:n]) if split else RAW[0][:, 0:n], None, j
            assert order[j] == (name, idx, c0, n, split)
            pump_dma()
            while st["split"] <= j or (st["split"] < len(order) and order[st["split"]][4]
                                       and st["split"] <= j + NSPL - 1
                                       and st["spl"] - NSPL < spl_slot.get(j, (0, 1 << 30))[1]
                                       and raw_ready.get(st["split"]) is not None):
                split_next()
            if split:
                slot = spl_slot[j][0]
                return (WH[slot][:, 0:n], WL[slot][:, 0:n]), split_ready[j], j
            return RAW[j % NRAW][:, 0:n], raw_ready[j], j

        def chunk_done(j, tok):
            if not order:
                return
            if order[j][4]:
                spl_free[spl_slot[j][1]] = tok
            else:
                raw_free[j] = tok
                pump_dma()

        def linear(parts, rhs, ranges, waits, per_k=True):
            slot, ps, free = pairs.take()
            total = sum(len(ks) for _, ks in parts)
            seen = 0
            for args, ks in parts:
                (hi, lo), ready, j = chunk(*args)
                for i, k in enumerate(ks):
                    xh, xl = rhs(k)
                    wk = waits[k] if per_k else waits
                    for a, n, c in ranges:
                        for q, (w, x) in enumerate(((hi, xh), (hi, xl), (lo, xh))):
                            last = q == 2 and k == ks[-1] and (a, n, c) == ranges[-1]
                            tok = MM(lambda e, w=w, x=x, i=i, a=a, n=n, c=c, s=(seen == 0 and q == 0),
                                     z=(seen == total - 1 and q == 2):
                                     e.matmul(ps[:, c:c + n], w[:, 128 * i:128 * i + 128], x[:, a:a + n],
                                              start=s, stop=z),
                                     ready, wk, free, inc=last)
                    seen += 1
                chunk_done(j, tok)
            return slot, ps, tok

        R768 = [(0, 512, 0), (512, 256, 512)]
        R512 = [(0, 512, 0)]

        def split_into(hi, lo, src, *w):
            a = A(lambda e: e.activation(hi, src, ACT.Copy), *w)
            b = V(lambda e: e.tensor_tensor(lo, src, hi.bitcast(F32), ALU.subtract), a, *w)
            return [a, b]

        CS = sb("CS", [128, 16])
        C4 = sb("C4", [128, 8, 4], F32R)
        C8 = sb("C8", [128, 8, 10])
        both = ExitStack()
        tmps = [sb(f"T{i}", [128, NT], F32, both) for i in range(6)]
        tmp = Ring(tmps)
        XC2 = sb("XC2", [128, 8, NCTX], F32, both)
        SMA = sb("SMA", [128, SM_1], F32, both)

        def xa(k, a0, n):
            return X[:, k, a0:a0 + n] if a0 < S else XC2[:, k, a0 - S:a0 - S + n]

        c_sm = [P.dma("sync", "sm", SMA[:, :], t["sm"][:, 0:SM_1]), P.dma("sync", "sm2", SM[:, :], t["sm"][:, SM_1:])]
        c_co = P.dma("sync", "co", CO[:, :], t["co"][:, :])
        g_eps = G(lambda e: e.memset(EPSC[:, :], EPS))
        first = ExitStack()
        MW = [sb(f"MW{i}", [128, NT], F32, first) for i in range(NMOD)]
        MH = [sb(f"MH{i}", [128, NT], F32R, first) for i in range(3)]
        ML = [sb(f"ML{i}", [128, NT], F32R, first) for i in range(3)]
        mwf, mhf, mwd = {}, {}, []

        def mod_load():
            i = len(mwd)
            if i < 32:
                mwd.append(P.dma("sync", f"mw{i % NMOD}", MW[i % NMOD][:, :], t["w_ada0"][i, :, :], mwf.get(i - NMOD)))


        x_done = []
        with ExitStack() as ph:
            XT = [sb(f"XT{i}", [128, 1024], F32, ph) for i in range(6)]
            xr = Ring(XT)
            for i in range(6):
                xs, xt, free = xr.take()
                src = t["x"][128 * i:128 * i + 128, :] if i < 4 else t["ctx"][128 * (i - 4):128 * (i - 4) + 128, :]
                d = P.dma("scalar", f"xt{xs}", xt[:, :], src, free)
                mod_load()
                slot, ps, pf = pairs.take()
                for k in range(8):
                    tok = MM(lambda e, k=k, xt=xt, ps=ps: e.transpose(ps[:, 128 * k:128 * k + 128], xt[:, 128 * k:128 * k + 128], ident),
                             d, c_co, pf, inc=(k == 7))
                xr.release(xs, tok)
                v = V(lambda e, i=i, ps=ps: e.tensor_copy(X[:, :, 128 * i:128 * i + 128] if i < 4 else XC2[:, :, 128 * i - S:128 * i - S + 128], ps.rearrange("p (k n) -> p k n", k=8)), tok)
                pairs.release(slot, v)
                x_done.append(v)
        cs = A(lambda e: e.activation(CS[:, :], sm("cc"), ACT.Silu), c_sm)
        cs3 = CS[:, :].rearrange("p (k q) -> p k q", k=8)
        cs = A(lambda e: e.activation(C4[:, :, 0:2], cs3, ACT.Copy), cs)
        cs = V(lambda e: e.tensor_tensor(C4[:, :, 2:4], cs3, C4[:, :, 0:2].bitcast(F32), ALU.subtract), cs)

        def rsqrt(ps, n, scale, w, *out_free):
            ysl, y, yf = tmp.take()
            vsl, v, vf = tmp.take()
            asl, a, af = tmp.take()
            hs = [slice(0, n // 2), slice(n // 2, n)]
            d = [V(lambda e: e.tensor_scalar(v[:, h], ps[:, h], scale, EPS, ALU.mult, ALU.add), w, vf) for h in hs]
            l = [A(lambda e: e.activation(y[:, h], v[:, h], ACT.Ln), t_, yf) for h, t_ in zip(hs, d)]
            l = [A(lambda e: e.activation(y[:, h], y[:, h], ACT.Exp, scale=-0.5), t_) for h, t_ in zip(hs, l)]
            x = [V(lambda e: e.scalar_tensor_tensor(a[:, h], y[:, h], -0.5, y[:, h], ALU.mult, ALU.mult), t_, af) for h, t_ in zip(hs, l)]
            x = [V(lambda e: e.tensor_tensor(a[:, h], a[:, h], v[:, h], ALU.mult), t_) for h, t_ in zip(hs, x)]
            x = [V(lambda e: e.scalar_tensor_tensor(y[:, h], a[:, h], 1.5, y[:, h], ALU.add, ALU.mult), t_) for h, t_ in zip(hs, x)]
            tmp.release(vsl, x)
            tmp.release(asl, x)
            return ysl, y, x, d

        class Squares:

            def __init__(self, ntok, ranges):
                self.ntok, self.ranges, self.known = ntok, ranges, None
                self.slot, self.ps, self.free = pairs.take()

            def add(self, k, wait):
                ps = self.ps
                ts, sq, tf = tmp.take()
                for a0, n, c in self.ranges:
                    a = A(lambda e: e.activation(sq[:, a0:a0 + n], xa(k, a0, n), ACT.Square), wait, tf)
                for a0, n, c in self.ranges:
                    tok = MM(lambda e: e.matmul(ps[:, c:c + n], ones, sq[:, a0:a0 + n], start=(k == 0), stop=(k == 7)), a, self.free, c_co)
                tmp.release(ts, tok)
                self.tok = tok

            def root(self):
                if self.known is None:
                    rs, ri, r, l = rsqrt(self.ps, self.ntok, 1.0 / 1024, self.tok)
                    pairs.release(self.slot, l)
                    self.known = rs, ri, r
                return self.known

        def rms(sqs, hh, hl, waits, scale_of, bias_of):
            rs, ri, r = sqs.root()
            ntok, ranges = sqs.ntok, sqs.ranges
            done = []
            held = []

            def low(k, ts, h, a, ranges=ranges):
                s = []
                for q, (a0, n, c) in enumerate(ranges):
                    bi, lo, hi = bias_of(k, q), hl[:, k, a0:a0 + n], hh[:, k, a0:a0 + n].bitcast(F32)
                    if bi is None:
                        s.append(V(lambda e: e.tensor_tensor(lo, h[:, a0:a0 + n], hi, ALU.subtract), a[q]))
                    else:
                        s.append(V(lambda e: e.scalar_tensor_tensor(lo, h[:, a0:a0 + n], bi, hi, ALU.add, ALU.subtract), a[q]))
                tmp.release(ts, s)
                done.append([a, s])

            for k in range(8):
                ts, h, tf = tmp.take()
                a = []
                for q, (a0, n, c) in enumerate(ranges):
                    bi = bias_of(k, q)
                    v = V(lambda e: e.scalar_tensor_tensor(h[:, a0:a0 + n], xa(k, a0, n), scale_of(k, q), ri[:, a0:a0 + n], ALU.mult, ALU.mult), r, tf, waits)
                    if bi is None:
                        a.append(A(lambda e: e.activation(hh[:, k, a0:a0 + n], h[:, a0:a0 + n], ACT.Copy), v))
                    else:
                        a.append(A(lambda e: e.activation(hh[:, k, a0:a0 + n], h[:, a0:a0 + n], ACT.Identity, bias=bi), v))
                if held:
                    low(*held.pop())
                held.append((k, ts, h, a))
            low(*held.pop())
            tmp.release(rs, done)
            return done

        def attention(steps):
            sring, lent = pairs.lend([0, 1, 2]), pairs.lend([3])
            oring = Ring([lent.items[0][:, 512 * i:512 * i + 512] for i in range(2)])
            oring.free = [lent.free[0], lent.free[0]]
            prob, prot = tmp.lend([0, 1, 2]), tmp.lend([3, 4])

            def first(s):
                slot, ps, free = sring.take()
                a, b = s["a"], s["b"]
                for kh, kl, c, n in s["ks"]:
                    MM(lambda e: e.matmul(ps[:, c:c + n], s["q"], kh, start=True, stop=False), free, s["wait"], inc=False)
                    tok = MM(lambda e: e.matmul(ps[:, c:c + n], s["ql"], kl, start=False, stop=True))
                if s["bias"] is not None:
                    tok = s["bias"](ps, tok)
                s.update(sslot=slot, sps=ps, tok=tok)

            def peak(s):
                a, b, ps, tok = s["a"], s["b"], s["sps"], s["tok"]
                ss, sv, sf = stat.take()
                m = V(lambda e: e.tensor_reduce(sv[:, 0:1], ps[:, a:b], AX.X, ALU.max, negate=True), tok, sf)
                if s["sink"] is not None:
                    m = V(lambda e: e.scalar_tensor_tensor(sv[:, 0:1], s["sink"], -1.0, sv[:, 0:1], ALU.mult, ALU.min), m)
                s.update(ss=ss, sv=sv, m=m)

            def expo(s):
                a, b, ps, sv = s["a"], s["b"], s["sps"], s["sv"]
                pslot, pr, pf = prob.take()
                x = A(lambda e: e.activation(pr[:, a:b], ps[:, a:b], ACT.Exp, bias=sv[:, 0:1]), s["m"], pf)
                es = None
                if s["sink"] is not None:
                    es = A(lambda e: e.activation(sv[:, 1:2], s["sink"], ACT.Exp, bias=sv[:, 0:1]), s["m"])
                s.update(pslot=pslot, pr=pr, x=x, es=es)

            def second(s):
                ps = s["sps"]
                nb = (s["b"] - s["a"]) // 128
                for i in range(nb):
                    c = s["a"] + 128 * i
                    tok = MM(lambda e, i=i, c=c: e.transpose(ps[:, 128 * i:128 * i + 128], s["pr"][:, c:c + 128], ident),
                             s["x"], inc=(i == nb - 1))
                prob.release(s["pslot"], tok)
                qslot, pt, qf = prot.take()
                n = 128 * nb
                na = min(n, 512)
                y = [A(lambda e: e.activation(pt[:, 0:na], ps[:, 0:na], ACT.Copy), tok, qf)]
                if n > na:
                    y.append(V(lambda e: e.tensor_copy(pt[:, na:n], ps[:, na:n]), tok, qf))
                sring.release(s["sslot"], y)
                s.update(qslot=qslot, pt=pt, y=y)

            def third(s):
                pt = s["pt"]
                s["tslot"], ps, free = oring.take()
                s["tps"] = ps
                n = len(s["vs"])
                for i, v in enumerate(s["vs"]):
                    tok = MM(lambda e, i=i, v=v: e.matmul(ps[:, 0:65], pt[:, 128 * i:128 * i + 128], v, start=(i == 0), stop=(i == n - 1)),
                             free, s["y"][0] if i < 4 else s["y"], s["vwait"], inc=(i == n - 1))
                prot.release(s["qslot"], tok)
                ss, sv = s["ss"], s["sv"]
                if s["es"] is not None:
                    d = V(lambda e: e.tensor_tensor(sv[:, 2:3], ps[:, 64:65], sv[:, 1:2], ALU.add), tok, s["es"])
                    d = V(lambda e: e.reciprocal(sv[:, 3:4], sv[:, 2:3]), d)
                else:
                    d = V(lambda e: e.reciprocal(sv[:, 3:4], ps[:, 64:65]), tok)
                s["d"] = d

            def finish(s):
                s["o"] = s["fin"](s["tps"][:, 0:64], s["sv"][:, 3:4], s["d"])
                stat.release(s["ss"], s["o"])
                if s["post"] is None:
                    oring.release(s["tslot"], s["o"])

            def after(s):
                if s["post"] is not None:
                    oring.release(s["tslot"], s["post"](s["tps"], s["o"]))

            n = len(steps)
            for i in range(n + 4):
                if i < n:
                    first(steps[i])
                if i >= 4:
                    finish(steps[i - 4])
                if 2 <= i < n + 2:
                    second(steps[i - 2])
                if i < n:
                    peak(steps[i])
                if 3 <= i < n + 3:
                    third(steps[i - 3])
                if i >= 4:
                    after(steps[i - 4])
                if i < n:
                    expo(steps[i])
            lent.free[0] = list(oring.free)
            pairs.give_back(sring, [0, 1, 2])
            pairs.give_back(lent, [3])
            tmp.give_back(prob, [0, 1, 2])
            tmp.give_back(prot, [3, 4])

        def stack_q(dst, ps, ntok, scale, w, at=0):
            a = A(lambda e: e.activation(dst[at:at + 64, 0:ntok], ps, ACT.Copy, scale=scale), w)
            v = V(lambda e: e.scalar_tensor_tensor(dst[64 - at:128 - at, 0:ntok], ps, scale, dst[at:at + 64, 0:ntok].bitcast(F32), ALU.mult, ALU.subtract), a)
            return [a, v]

        def stack_k(dh, dl, ps, ntok, w):
            a = [A(lambda e: e.activation(dh[64 * f:64 * f + 64, 0:ntok], ps, ACT.Copy), w) for f in range(2)]
            v = [V(lambda e: e.scalar_tensor_tensor(dl[64 * f:64 * f + 64, 0:ntok], ps, 1.0, dh[64 * f:64 * f + 64, 0:ntok].bitcast(F32), ALU.mult, ALU.subtract), a) for f in range(2)]
            return [a, v]

        def pair_k(dh, dl, ps, ntok, at, w):
            a = [A(lambda e: e.activation(dh[64 * f:64 * f + 64, 0:ntok], ps, ACT.Copy), w) for f in range(2)]
            v = V(lambda e: e.scalar_tensor_tensor(dl[at:at + 64, 0:ntok], ps, 1.0, dh[at:at + 64, 0:ntok].bitcast(F32), ALU.mult, ALU.subtract), a)
            return [a, v]

        ap_ = sm("a_param")
        v = V(lambda e: e.scalar_tensor_tensor(C8[:, 0, :], ap_, -1.0, ap_, ALU.mult, ALU.max), c_sm)
        a = A(lambda e: e.activation(C8[:, 1, :], C8[:, 0, :], ACT.Exp, scale=-1.0), v)
        v = V(lambda e: e.tensor_scalar(C8[:, 2, :], C8[:, 1, :], 2.0, None, ALU.add), a)
        v = V(lambda e: e.reciprocal(C8[:, 3, :], C8[:, 2, :]), v)
        v = V(lambda e: e.tensor_tensor(C8[:, 2, :], C8[:, 1, :], C8[:, 3, :], ALU.mult), v)
        v = V(lambda e: e.tensor_tensor(C8[:, 3, :], C8[:, 2, :], C8[:, 2, :], ALU.mult), v)
        v = V(lambda e: e.tensor_scalar(C8[:, 4, :], C8[:, 3, :], 1.0 / 19, 1.0 / 17, ALU.mult, ALU.add), v)
        for n in (15, 13, 11, 9, 7, 5, 3, 1):
            v = V(lambda e: e.tensor_tensor(C8[:, 4, :], C8[:, 4, :], C8[:, 3, :], ALU.mult), v)
            v = V(lambda e, n=n: e.tensor_scalar(C8[:, 4, :], C8[:, 4, :], 1.0 / n, None, ALU.add), v)
        v = V(lambda e: e.scalar_tensor_tensor(C8[:, 4, :], C8[:, 4, :], 2.0, C8[:, 2, :], ALU.mult, ALU.mult), v)
        v = V(lambda e: e.tensor_scalar(C8[:, 5, :], ap_, -1.0, 0.0, ALU.mult, ALU.max), v)
        v = V(lambda e: e.tensor_tensor(C8[:, 5, :], C8[:, 5, :], C8[:, 4, :], ALU.add), v)
        c8 = V(lambda e: e.tensor_scalar(C8[:, 6, :], C8[:, 5, :], -8.0, None, ALU.mult), v)
        sqs = Squares(NT, R768)
        for k in range(8):
            sqs.add(k, x_done)
        sqs.root()
        mod1 = []
        macc = {}
        for _ in range(NMOD - 6):
            mod_load()

        def mod_first(i):
            src, hi, lo, k, ps = MW[i % NMOD][:, :], MH[i % 3][:, :], ML[i % 3][:, :], i % 8, macc["ps"]
            a = A(lambda e: e.activation(hi, src, ACT.Copy), mwd[i], mhf.get(i - 3))
            b = V(lambda e: e.tensor_tensor(lo, src, hi.bitcast(F32), ALU.subtract), a)
            mwf[i] = b
            for q, w in enumerate((hi, lo)):
                for a0, n, o in R768:
                    tok = MM(lambda e: e.matmul(ps[0:4, o:o + n], C4[:, k, :], w[:, a0:a0 + n], start=(k == 0 and q == 0), stop=(k == 7 and q == 1)),
                             b, cs, macc["free"])
            mhf[i] = tok
            macc["tok"] = tok
            mod_load()
            if len(mwd) == 32:
                pump_dma()


        def mod_begin(L, c):
            macc["slot"], macc["ps"], macc["free"] = pairs.take()

        def mod_part(L, c, k, how):
            (hi, lo), ready, j = chunk(f"w_ada{L}", 8 * c + k, 0, 768, how)
            ps = macc["ps"]
            for q, w in enumerate((hi, lo)):
                for a0, n, o in R768:
                    tok = MM(lambda e: e.matmul(ps[0:4, o:o + n], C4[:, k, :], w[:, a0:a0 + n], start=(k == 0 and q == 0), stop=(k == 7 and q == 1)),
                             ready, cs, macc["free"])
            chunk_done(j, tok)
            macc["tok"] = tok

        def mod_end(L, c):
            ts, row, tf = tmp.take()
            a = A(lambda e: e.activation(row[0:4, 0:NT], macc["ps"][0:4, 0:NT], ACT.Copy), macc["tok"], tf)
            pairs.release(macc["slot"], a)
            slot, ps, free = pairs.take()
            for m in range(6):
                tok = MM(lambda e: e.transpose(ps[:, 4 * m:4 * m + 4], row[0:4, 128 * m:128 * m + 128], ident[0:4, 0:4]), a, free)
            tmp.release(ts, tok)
            p3 = ps[:, 0:24].rearrange("p (m q) -> p m q", m=6)
            dst = MODS[L][:, 6 * c:6 * c + 6, :]
            v = V(lambda e: e.tensor_tensor(dst, p3[:, :, 0:2], sm(f"b_ada{L}", 6 * c, 6).unsqueeze(2).broadcast_to([128, 6, 2]), ALU.add), tok, c_sm)
            v = V(lambda e: e.tensor_tensor(dst, dst, p3[:, :, 2:4], ALU.add), v)
            pairs.release(slot, v)
            return v

        def mod_ticks():
            for c in range(4):
                mod_begin(1, c)
                for k in range(8):
                    mod_part(1, c, k, 2)
                    if k == 7:
                        mod1.append(mod_end(1, c))
                    yield

        mticks = mod_ticks()

        def mod_tick(n):
            for _ in range(n):
                next(mticks, None)

        for L in range(2):
            lay = ExitStack()
            ntk = NT if L == 0 else S
            rx = R768 if L == 0 else R512
            if L == 0:
                mdt = []
                for c in range(4):
                    mod_begin(0, c)
                    for k in range(8):
                        mod_first(8 * c + k)
                    mdt.append(mod_end(0, c))
                if order:
                    split_next()
                    split_next()
                first.close()
                fenced = P.now()
            MOD = MODS[L]
            for q in range(2):
                a = V(lambda e, q=q: e.scalar_tensor_tensor(AB[:, :, q], MOD[:, 8:16, q], 1.0, sm(f"norm_g{L}"), ALU.add, ALU.mult), mdt)
            Hh = sb(f"Hh{L}", [128, 8, NT], F32R, lay)
            Hl = sb(f"Hl{L}", [128, 8, NT], F32R, lay)
            hd = rms(sqs, Hh, Hl, [a, x_done, fenced], lambda k, q: AB[:, k, q:q + 1], lambda k, q: MOD[:, k, q:q + 1])
            Y = sb(f"Y{L}", [128, 8, ntk], F32, lay)
            ydone = [None] * 8

            def win(col, ranges, L=L, hd=hd, Hh=Hh, Hl=Hl):
                return linear([((f"w_in{L}", col // 128, 0, 1024), list(range(8)))],
                              lambda k: (Hh[:, k, :], Hl[:, k, :]), ranges, hd)

            def merge(branch, wname, Gh, Gl, gdone, L=L, ntk=ntk, rx=rx, Y=Y, ydone=ydone, win=win):
                for m in range(8):
                    s1, p1, t1 = win(4864 + 1024 * branch + 128 * m, rx)
                    ts, sg, tf = tmp.take()
                    g = A(lambda e, sg=sg, p1=p1: e.activation(sg[:, 0:ntk], p1[:, 0:ntk], ACT.Sigmoid), t1, tf)
                    pairs.release(s1, g)
                    s2, p2, t2 = linear([((f"{wname}{L}", m, 0, 512), [0, 1, 2, 3])],
                                        lambda k: (Gh[:, k, :], Gl[:, k, :]), rx, gdone)
                    if branch == 0:
                        y = V(lambda e, m=m, sg=sg, p2=p2: e.tensor_tensor(Y[:, m, :], sg[:, 0:ntk], p2[:, 0:ntk], ALU.mult), t2, g)
                        pairs.release(s2, y)
                    else:
                        y = V(lambda e, sg=sg, p2=p2: e.tensor_tensor(sg[:, 0:ntk], sg[:, 0:ntk], p2[:, 0:ntk], ALU.mult), t2, g)
                        pairs.release(s2, y)
                        y = V(lambda e, m=m, sg=sg: e.tensor_tensor(Y[:, m, :], Y[:, m, :], sg[:, 0:ntk], ALU.add), y, ydone[m])
                    tmp.release(ts, y)
                    ydone[m] = y

            def conv_branch(L=L, ntk=ntk, rx=rx, Y=Y, win=win):
                with ExitStack() as ph:
                    C = sb(f"C{L}", [128, 4, ntk], F32, ph)
                    SG = sb(f"SG{L}", [128, 4, ntk], F32, ph)
                    ip = ExitStack()
                    AP_ = [sb(f"AP{L}{i}", [128, NT + 60 if L == 0 else S + 30], F32, ip) for i in range(4)]
                    segs = [(0, 512, 15)] + ([(512, 256, 15 + 512 + 30)] if L == 0 else [])
                    now = P.now()
                    z = [G(lambda e: e.memset(ap[:, :], 0.0), now) for ap in AP_]
                    cd = [None] * 4
                    ready = [None] * 4
                    cw = SM_AT[f"conv_w{L}"][0]

                    def taps():
                        for group in (((0,), (1,), (2,), (3,)) if L == 0 else ((0, 1), (2, 3))):
                            ys = {}
                            for k in range(31):
                                for m in group:
                                    for a0, n, o in segs:
                                        src, w = AP_[m][:, o - 15 + k:o - 15 + k + n], smc(cw + 31 * m + k, cw + 31 * m + k + 1)
                                        if k == 0:
                                            ys[m, a0] = V(lambda e: e.tensor_scalar(C[:, m, a0:a0 + n], src, w, sm(f"conv_b{L}", m, 1), ALU.mult, ALU.add), ready[m])
                                        else:
                                            ys[m, a0] = V(lambda e: e.scalar_tensor_tensor(C[:, m, a0:a0 + n], src, w, C[:, m, a0:a0 + n], ALU.mult, ALU.add), ys[m, a0])
                                    if k == 30:
                                        cd[m] = [ys[m, a0] for a0, n, o in segs]
                                yield

                    tg = taps()

                    def some(n):
                        for _ in range(n):
                            next(tg, None)

                    for m in range(4):
                        s1, p1, t1 = win(512 + 128 * m, rx)
                        if L == 0:
                            mod_tick(1)
                        if m > L:
                            some(7)
                        ts, sg, tf = tmp.take()
                        g = A(lambda e: e.activation(sg[:, 0:ntk], p1[:, 0:ntk], ACT.Sigmoid), t1, tf)
                        pairs.release(s1, g)
                        s2, p2, t2 = win(128 * m, rx)
                        if L == 0:
                            mod_tick(1)
                        if m > L:
                            some(7)
                        ap = AP_[m]
                        ready[m] = [V(lambda e: e.tensor_tensor(ap[:, o:o + n], sg[:, a0:a0 + n], p2[:, a0:a0 + n], ALU.mult), t2, g, z)
                                    for a0, n, o in segs]
                        pairs.release(s2, ready[m])
                        tmp.release(ts, ready[m])
                    sgd = []
                    for m in range(8):
                        s1, p1, t1 = win(4864 + 128 * m, rx)
                        g = A(lambda e: e.activation(Y[:, m, :], p1[:, 0:ntk], ACT.Sigmoid), t1)
                        pairs.release(s1, g)
                        sgd.append(g)
                        some(7 if L == 0 else 3)
                        if L == 0:
                            mod_tick(1)
                    sgs = []
                    for m in range(4):
                        s1, p1, t1 = win(1024 + 128 * m, rx)
                        sgs.append(A(lambda e: e.activation(SG[:, m, :], p1[:, 0:ntk], ACT.Silu), t1))
                        pairs.release(s1, sgs[m])
                        some(7 if L == 0 else 3)
                        if L == 0:
                            mod_tick(1)
                    some(124)
                    yf = P.barrier()
                    ip.close()
                    Gh = sb(f"CGh{L}", [128, 4, ntk], F32R, ph)
                    Gl = sb(f"CGl{L}", [128, 4, ntk], F32R, ph)
                    s1, p1, pf = pairs.take()
                    for m in range(4):
                        for a0, n, c in rx:
                            tok = MM(lambda e: e.matmul(p1[:, c:c + n], ones, C[:, m, a0:a0 + n], start=(m == 0), stop=(m == 3)), cd[m], pf)
                    if L == 0:
                        mod_tick(6)
                    cs2 = [V(lambda e: e.scalar_tensor_tensor(C[:, m, :], p1[:, 0:ntk], -1.0 / 512, C[:, m, :], ALU.mult, ALU.add), tok) for m in range(4)]
                    pairs.release(s1, cs2)
                    s1, p1, pf = pairs.take()
                    for m in range(4):
                        ts, sq, tf = tmp.take()
                        a = A(lambda e: e.activation(sq[:, 0:ntk], C[:, m, :], ACT.Square), cs2[m], tf)
                        for a0, n, c in rx:
                            tok = MM(lambda e: e.matmul(p1[:, c:c + n], ones, sq[:, a0:a0 + n], start=(m == 0), stop=(m == 3)), a, pf)
                        tmp.release(ts, tok)
                    rs, ri, r, l = rsqrt(p1, ntk, 1.0 / 512, tok)
                    pairs.release(s1, l)
                    if L == 0:
                        mod_tick(6)
                    gd = [None] * 4
                    lns = []
                    for m in range(4):
                        y = V(lambda e: e.tensor_tensor(C[:, m, :], C[:, m, :], ri[:, 0:ntk], ALU.mult), r)
                        lns.append(A(lambda e: e.activation(C[:, m, :], C[:, m, :], ACT.Silu, bias=sm(f"cln_b{L}", m, 1), scale=sm(f"cln_g{L}", m, 1)), y))
                    tmp.release(rs, y)
                    for m in range(5):
                        if m < 4:
                            y2 = V(lambda e: e.tensor_tensor(SG[:, m, :], SG[:, m, :], C[:, m, :], ALU.mult), sgs[m], lns[m])
                            hi = A(lambda e: e.activation(Gh[:, m, :], SG[:, m, :], ACT.Copy), y2)
                        if m:
                            gd[m - 1] = [was, V(lambda e: e.tensor_tensor(Gl[:, m - 1, :], SG[:, m - 1, :], Gh[:, m - 1, :].bitcast(F32), ALU.subtract), was)]
                        was = hi
                    for m in range(8):
                        s2, p2, t2 = linear([((f"w_proj_a{L}", m, 0, 512), [0, 1, 2, 3])],
                                            lambda k: (Gh[:, k, :], Gl[:, k, :]), rx, gd)
                        y = V(lambda e: e.tensor_tensor(Y[:, m, :], Y[:, m, :], p2[:, 0:ntk], ALU.mult), t2, sgd[m])
                        pairs.release(s2, y)
                        ydone[m] = y
                P.barrier()

            def attn_branch(br, L=L, ntk=ntk, rx=rx, Y=Y, win=win):
                wa = br == 1
                cq, ck, cv, cg = (3584, 4096, 4224, 4352) if wa else (1536, 2048, 2560, 3072)
                with ExitStack() as ph:
                    O = sb(f"O{L}{br}", [128, 4, ntk], F32, ph)
                    inner = ExitStack()
                    nq, nk, nl, nv = (8, 2, 1, 2) if wa else (4, 4, 2, 4)
                    Q = sb(f"Q{L}{br}", [128, nq, ntk], F32R, inner)
                    KH = sb(f"KH{L}{br}", [128, nk, NT], F32R, inner)
                    KL = sb(f"KL{L}{br}", [128, nl, NT], F32R, inner)
                    VV = sb(f"V{L}{br}", [128, 6, nv, 65], F32, inner)
                    QG = sb(f"QG{L}{br}", [128, 1], F32, inner)
                    now = P.now()
                    rope = []
                    if wa:
                        RC = O[:, :, :].rearrange("p m n -> p (m n)")[:, 0:1024]
                        MK = sb(f"MK{L}", [128, 384], F32, inner)
                        rope = [P.dma("sync", "rc", RC[:, :], t["rope"][:, :], now),
                                P.dma("sync", "mk", MK[:, :], t["wmask"][:, :], now)]
                    else:
                        BI = sb(f"BI{L}", [128, 512], F32, inner)
                    vone = G(lambda e: e.memset(VV[:, :, :, 64:65], 1.0), now)
                    qg = V(lambda e: e.tensor_scalar(QG[:, :], sm(f"wa_q{L}" if wa else f"na_q{L}"), 0.125, None, ALU.mult))
                    vdone = [vone]

                    def normed(col, ranges, n, gain, store, got, pre):
                        s1, p1, t1 = win(col, ranges)
                        ts, q0, tf = tmp.take()
                        us, sq, uf = tmp.take()
                        c0, a = [], []
                        for a0, m, c in ranges:
                            c0.append(V(lambda e: e.tensor_copy(q0[:, a0:a0 + m], p1[:, a0:a0 + m]), t1, tf))
                            a.append(A(lambda e: e.activation(sq[:, a0:a0 + m], q0[:, a0:a0 + m], ACT.Square), c0, uf))
                        pairs.release(s1, c0)
                        yield
                        s2, p2, pf = pairs.take()
                        for a0, m, c in ranges:
                            tok = MM(lambda e: e.matmul(p2[:, c:c + m], bones, sq[:, a0:a0 + m], start=True, stop=True), a, pf)
                        tmp.release(us, tok)
                        us, sq, r, l = rsqrt(p2, n, 1.0 / 64, tok)
                        if not wa:
                            y = [V(lambda e: e.scalar_tensor_tensor(p2[:, a0:a0 + m], q0[:, a0:a0 + m], gain, sq[:, a0:a0 + m], ALU.mult, ALU.mult), r, qg) for a0, m, c in ranges]
                            tmp.release(us, y)
                            tmp.release(ts, y)
                            outs = [store(p2, w, pre, a0, m) for w, (a0, m, c) in zip(y, ranges)]
                            pairs.release(s2, outs)
                            got.append(outs)
                            return
                        pairs.release(s2, l)
                        y = V(lambda e: e.scalar_tensor_tensor(q0[:, 0:n], q0[:, 0:n], gain, sq[:, 0:n], ALU.mult, ALU.mult), r, qg)
                        yield
                        s3, p3, pf = pairs.take()
                        tok = MM(lambda e: e.matmul(p3[:, 0:S], rmat, q0[:, 0:S], start=True, stop=True), y, pf)
                        b = V(lambda e: e.tensor_tensor(sq[:, 0:S], p3[:, 0:S], RC[:, S:2 * S], ALU.mult), tok, y, rope)
                        c2 = V(lambda e: e.tensor_copy(p3[:, S:n], q0[:, S:n]), y, pf) if n > S else None
                        c1 = V(lambda e: e.tensor_tensor(q0[:, 0:S], q0[:, 0:S], RC[:, 0:S], ALU.mult), tok, rope)
                        y = V(lambda e: e.tensor_tensor(p3[:, 0:S], q0[:, 0:S], sq[:, 0:S], ALU.add), b, c1)
                        tmp.release(us, y)
                        tmp.release(ts, y)
                        outs = [store(p3, w, pre, a0, m) for w, (a0, m, c) in zip((y, c2), ranges)]
                        pairs.release(s3, outs)
                        got.append(outs)

                    def values(m, dst, pre):
                        s1, p1, t1 = win(cv + 128 * m, R768)
                        ts, vf, tf = tmp.take()
                        a = A(lambda e: e.activation(vf[:, :], p1[:, 0:NT], ACT.Copy), t1, tf)
                        pairs.release(s1, a)
                        yield
                        s2, p2, pf = pairs.take()
                        for i in range(6):
                            tok = MM(lambda e: e.transpose(p2[:, 128 * i:128 * i + 128], vf[:, 128 * i:128 * i + 128], ident), a, pf, inc=(i == 5))
                        tmp.release(ts, tok)
                        y = V(lambda e: e.tensor_copy(VV[:, :, dst:dst + 2, 0:64], p2[:, 0:768].rearrange("p (i h d) -> p i h d", i=6, h=2)), tok, pre)
                        pairs.release(s2, y)
                        vdone.append(y)

                    for part in range(1 if wa else 2):
                        qdone, kdone = [], []
                        pre = P.now()
                        tasks = []
                        kgain = sm(f"wa_k{L}" if wa else f"na_k{L}")
                        if wa:
                            tasks.append(normed(ck, R768, NT, kgain,
                                                lambda ps, w, pre, a, n: [pair_k(KH[:, f, a:a + n], KL[:, 0, a:a + n], ps[64 * f:64 * f + 64, a:a + n], n, 64 * f, [w, pre]) for f in range(2)], kdone, pre))
                        else:
                            for m in range(2):
                                tasks.append(normed(ck + 128 * (2 * part + m), R768, NT, kgain,
                                                    lambda ps, w, pre, a, n, m=m: [pair_k(KH[:, 2 * m + f, a:a + n], KL[:, m, a:a + n], ps[64 * f:64 * f + 64, a:a + n], n, 64 * f, [w, pre]) for f in range(2)], kdone, pre))
                        for m in range(4 if wa else 2):
                            tasks.append(normed(cq + 128 * (2 * part + m), rx, ntk, QG[:, 0:1],
                                                lambda ps, w, pre, a, n, m=m: [stack_q(Q[:, 2 * m + f, a:a + n], ps[64 * f:64 * f + 64, a:a + n], n, 1.0, [w, pre], 64 * (m // 2) if wa else 64 * f) for f in range(2)], qdone, pre))
                        tasks += [values(0, 0, pre)] if wa else [values(2 * part + m, 2 * m, pre) for m in range(2)]
                        pipeline(tasks)

                        steps = []
                        lent = tmp.lend([5])
                        t5, f5 = tmps[5], list(lent.free[0])
                        oring = Ring([t5[:, 0:256], t5[:, 256:512]] if wa else [t5[:, 0:256]])
                        oring.free = [list(f5) for _ in oring.items]
                        if not wa:
                            bring = Ring([t5[:, 256:768], BI[:, :]])
                            bring.free = [list(f5), [pre]]
                        for half, qt in [(f, q) for f in (range(2) if wa else [part]) for q in range(6 if L == 0 else 4)]:
                            isx = qt < 4
                            box = {}
                            for h in range(4):
                                head = 4 * half + h
                                qh, kt, vh = (head, half, half) if wa else (h, h, h)
                                r0 = 64 * (half if wa else h % 2)
                                r1 = r0 + 64
                                kl = KL[r0:r1, 0 if wa else h // 2, :]
                                if not isx:
                                    lo_t, nw = 0, 0
                                elif wa:
                                    lo_t = max(qt - 1, 0)
                                    nw = 128 * (min(qt + 2, 4) - lo_t)
                                else:
                                    lo_t, nw = 0, 512
                                ks = [(KH[:, kt, 128 * lo_t:128 * lo_t + nw], kl[:, 128 * lo_t:128 * lo_t + nw], 512 - nw, nw)] if nw else []
                                ks.append((KH[:, kt, 512:768], kl[:, 512:768], 512, 256))
                                vs = [VV[:, lo_t + i, vh, :] for i in range(nw // 128)] + [VV[:, 4 + i, vh, :] for i in range(2)]

                                def bias(ps, tok, head=head, qt=qt, nw=nw, lo_t=lo_t):
                                    if wa:
                                        o = 128 * (lo_t - (qt - 1))
                                        return V(lambda e: e.tensor_tensor(ps[:, 512 - nw:512], ps[:, 512 - nw:512], MK[:, o:o + nw], ALU.add), tok, rope)
                                    bs, bt, bf = bring.take()
                                    d = P.dma("gpsimd", f"bi{bs}", bt[:, :], t[f"rpb{L}"][head, :, 64 * (7 - 2 * qt):64 * (7 - 2 * qt) + 512], bf, pre)
                                    y = V(lambda e: e.tensor_tensor(ps[:, 0:512], ps[:, 0:512], bt[:, :], ALU.add), tok, d)
                                    bring.release(bs, y)
                                    return y

                                def fin(o, r, d, h=h, box=box):
                                    if h == 0:
                                        box["slot"], box["o"], box["free"] = oring.take()
                                    ot = box["o"]
                                    y = V(lambda e: e.tensor_scalar(ot[:, 64 * h:64 * h + 64], o, r, None, ALU.mult), d, box["free"])
                                    box["done"] = y
                                    return y

                                def post(ps, free, qt=qt, box=box, half=half):
                                    for i in range(2):
                                        tok = MM(lambda e: e.transpose(ps[:, 128 * i + 128:128 * i + 256], box["o"][:, 128 * i:128 * i + 128], ident), free, box["done"], inc=(i == 1))
                                    oring.release(box["slot"], tok)
                                    return V(lambda e: e.tensor_copy(O[:, 2 * half:2 * half + 2, 128 * qt:128 * qt + 128], ps[:, 128:384].rearrange("p (m n) -> p m n", m=2)), tok)

                                steps.append(dict(q=Q[:, qh, 128 * qt:128 * qt + 128], ql=Q[r0:r1, qh, 128 * qt:128 * qt + 128], ks=ks, a=512 - nw, b=768,
                                                  bias=bias if isx else None, sink=sm(f"sink{L}", head, 1) if wa else None,
                                                  vs=vs, fin=fin, post=post if h == 3 else None,
                                                  wait=[qdone[qh // 2], kdone[0 if wa else h // 2], pre],
                                                  vwait=vdone))
                        attention(steps)
                        lent.free[0] = [oring.free, [] if wa else bring.free]
                        tmp.give_back(lent, [5])
                    inner.close()
                    done = P.now()
                    Gh = sb(f"Gh{L}{br}", [128, 4, ntk], F32R, ph)
                    Gl = sb(f"Gl{L}{br}", [128, 4, ntk], F32R, ph)
                    gd = []
                    for m in range(4):
                        s1, p1, t1 = win(cg + 128 * m, rx)
                        ts, sg, tf = tmp.take()
                        g = A(lambda e: e.activation(sg[:, 0:ntk], p1[:, 0:ntk], ACT.Silu), t1, tf)
                        pairs.release(s1, g)
                        y = V(lambda e: e.tensor_tensor(sg[:, 0:ntk], sg[:, 0:ntk], O[:, m, :], ALU.mult), g)
                        s = split_into(Gh[:, m, :], Gl[:, m, :], sg[:, 0:ntk], y, done)
                        tmp.release(ts, s)
                        gd.append(s)
                    merge(1 + br, "w_proj_c" if wa else "w_proj_b", Gh, Gl, gd)
                P.barrier()

            conv_branch()
            attn_branch(0)
            attn_branch(1)

            yd = [split_into(Hh[:, k, 0:ntk], Hl[:, k, 0:ntk], Y[:, k, :], ydone[k]) for k in range(8)]
            x_done = []
            mdt = mod1
            sqs = Squares(NT, R768) if L == 0 else Squares(S, R512)
            for m in range(8):
                s1, p1, t1 = linear([((f"w_o{L}", m, 0, 1024), list(range(8)))], lambda k: (Hh[:, k, :], Hl[:, k, :]), rx, yd)
                ys = [V(lambda e, m=m, q=q, a0=a0, n=n, p1=p1: e.scalar_tensor_tensor(xa(m, a0, n), p1[:, a0:a0 + n], MOD[:, 16 + m, q:q + 1], xa(m, a0, n), ALU.mult, ALU.add), t1)
                      for q, (a0, n, c) in enumerate(rx)]
                pairs.release(s1, ys)
                x_done.append(ys)
                if m:
                    sqs.add(m - 1, x_done[m - 1])
            sqs.add(7, x_done[7])
            lay.close()
            P.barrier()

        both.close()
        tmps = [sb(f"U{i}", [128, 516]) for i in range(6)]
        tmp = Ring(tmps)

        def plain_rms(name, sqs, hh, hl, waits):
            return rms(sqs, hh, hl, waits, lambda k, q: sm(name, k, 1), lambda k, q: None)

        def add_out(name, nkt, parts_of, gh, gl, gdone):
            res = []
            sqs = Squares(S, R512)
            for m in range(8):
                s1, p1, t1 = linear(parts_of(m), lambda k: (gh[:, k, :], gl[:, k, :]), R512, gdone)
                y = V(lambda e, m=m, p1=p1: e.tensor_tensor(X[:, m, 0:S], X[:, m, 0:S], p1[:, 0:S], ALU.add), t1)
                pairs.release(s1, y)
                res.append(y)
                if m:
                    sqs.add(m - 1, res[m - 1])
            sqs.add(7, res[7])
            return sqs, res

        def ffn(idx, sqs, x_done):
            with ExitStack() as ph:
                Gh = sb(f"FGh{idx}", [128, 24, S], F32R, ph)
                Gl = sb(f"FGl{idx}", [128, 24, S], F32R, ph)
                gd = []
                with ExitStack() as p2_:
                    Hh = sb(f"FHh{idx}", [128, 8, S], F32R, p2_)
                    Hl = sb(f"FHl{idx}", [128, 8, S], F32R, p2_)
                    hd = plain_rms(f"ffn_norm{idx}", sqs, Hh, Hl, x_done)
                    cw, cb = SM_AT[f"ffn_cw{idx}"][0], SM_AT[f"ffn_cb{idx}"][0]
                    for m in range(24):
                        s1, p1, t1 = linear([((f"ffn_in{idx}", m, 0, 1024), list(range(8)))], lambda k: (Hh[:, k, :], Hl[:, k, :]), R512, hd)
                        ts, pa, tf = tmp.take()
                        z = V(lambda e, pa=pa: e.memset(pa[:, 0:2], 0.0), tf)
                        a = A(lambda e, pa=pa, p1=p1: e.activation(pa[:, 2:2 + S], p1[:, 0:S], ACT.Copy), t1, tf)
                        pairs.release(s1, a)
                        us, u, uf = tmp.take()
                        y = V(lambda e, m=m, pa=pa, u=u: e.tensor_scalar(u[:, 0:S], pa[:, 0:S], smc(cw + 3 * m, cw + 3 * m + 1), smc(cb + m, cb + m + 1), ALU.mult, ALU.add), a, z, uf)
                        for k in (1, 2):
                            y = V(lambda e, m=m, k=k, pa=pa, u=u: e.scalar_tensor_tensor(u[:, 0:S], pa[:, k:k + S], smc(cw + 3 * m + k, cw + 3 * m + k + 1), u[:, 0:S], ALU.mult, ALU.add), y)
                        tmp.release(ts, y)
                        g = A(lambda e, u=u: e.activation(u[:, 0:S], u[:, 0:S], ACT.Gelu_apprx_tanh), y)
                        s2, p2, t2 = linear([((f"ffn_in{idx}", 24 + m, 0, 1024), list(range(8)))], lambda k: (Hh[:, k, :], Hl[:, k, :]), R512, hd)
                        y = V(lambda e, u=u, p2=p2: e.tensor_tensor(u[:, 0:S], u[:, 0:S], p2[:, 0:S], ALU.mult), g, t2)
                        pairs.release(s2, y)
                        s = split_into(Gh[:, m, :], Gl[:, m, :], u[:, 0:S], y)
                        tmp.release(us, s)
                        gd.append(s)
                res = add_out("ffn_out", 24, lambda m: [((f"ffn_out{idx}", m, 1024 * c, 1024), list(range(8 * c, 8 * c + 8))) for c in range(3)], Gh, Gl, gd)
            P.barrier()
            return res

        def lru(sqs, x_done, ph):
            RG = sb("RG", [128, 10, S], F32, ph)
            IG = sb("IG", [128, 10, S], F32, ph)
            Gh = sb("LGh", [128, 10, S], F32R, ph)
            Gl = sb("LGl", [128, 10, S], F32R, ph)
            with ExitStack() as p2_:
                Hh = sb("LHh", [128, 8, S], F32R, p2_)
                Hl = sb("LHl", [128, 8, S], F32R, p2_)
                XS = [sb(f"XS{i}", [128, 2, S], F32R, p2_) for i in range(3)]
                xsr = Ring(XS)
                hd = plain_rms("lru_norm", sqs, Hh, Hl, x_done)

                def lru_in(m):
                    return linear([(("lru_in", m, 0, 1024), list(range(8)))], lambda k: (Hh[:, k, :], Hl[:, k, :]), R512, hd)

                cw = SM_AT["lru_conv_w"][0]
                rec = [None] * 10

                def recur(m):
                    s1, p1, t1 = lru_in(10 + m)
                    ts, pa, tf = tmp.take()
                    z = V(lambda e: e.memset(pa[:, 0:3], 0.0), tf)
                    a = A(lambda e: e.activation(pa[:, 3:3 + S], p1[:, 0:S], ACT.Copy), t1, tf)
                    pairs.release(s1, a)
                    us, xc, uf = tmp.take()
                    y = V(lambda e: e.tensor_scalar(xc[:, 0:S], pa[:, 0:S], smc(cw + 4 * m, cw + 4 * m + 1), sm("lru_conv_b", m, 1), ALU.mult, ALU.add), a, z, uf)
                    for k in (1, 2, 3):
                        y = V(lambda e: e.scalar_tensor_tensor(xc[:, 0:S], pa[:, k:k + S], smc(cw + 4 * m + k, cw + 4 * m + k + 1), xc[:, 0:S], ALU.mult, ALU.add), y)
                    tmp.release(ts, y)
                    xslot, xs, xf = xsr.take()
                    s = split_into(xs[:, 0, :], xs[:, 1, :], xc[:, 0:S], y, xf)
                    yield
                    yield
                    (hi, lo), ready, j = chunk("gate_w", m, 0, 256)
                    pslot, pp, pf = pairs.take()
                    for g in range(2):
                        for q, (w, xi) in enumerate(((hi, 0), (hi, 1), (lo, 0))):
                            tok = MM(lambda e: e.matmul(pp[:, 512 * g:512 * g + 512], w[:, 128 * g:128 * g + 128], xs[:, xi, :], start=(q == 0), stop=(q == 2)),
                                     ready, s, pf, inc=(q == 2))
                    chunk_done(j, tok)
                    xsr.release(xslot, tok)
                    a1 = A(lambda e: e.activation(RG[:, m, :], pp[:, 0:S], ACT.Sigmoid, bias=sm("gate_b", m, 1)), tok)
                    a2 = A(lambda e: e.activation(IG[:, m, :], pp[:, 512:1024], ACT.Sigmoid, bias=sm("gate_b", 10 + m, 1)), tok)
                    pairs.release(pslot, a1, a2)
                    i1 = V(lambda e: e.tensor_tensor(IG[:, m, :], IG[:, m, :], xc[:, 0:S], ALU.mult), a2)
                    tmp.release(us, i1)
                    u = V(lambda e: e.tensor_scalar(RG[:, m, :], RG[:, m, :], C8[:, 6, m:m + 1], None, ALU.mult), a1, c8)
                    rec[m] = (u, i1)

                def scans(group):
                    th = {}
                    for m in group:
                        ts, h, tf = tmp.take()
                        a = A(lambda e: e.activation(h[:, 0:S], RG[:, m, :], ACT.Tanh, scale=-1.0), rec[m], tf)
                        x = A(lambda e: e.activation(RG[:, m, :], RG[:, m, :], ACT.Exp), a)
                        vs, v, vf = tmp.take()
                        y = V(lambda e: e.tensor_tensor(v[:, 0:S], RG[:, m, :], RG[:, m, :], ALU.mult), x, vf)
                        y = V(lambda e: e.scalar_tensor_tensor(h[:, 0:S], v[:, 0:S], 1.0, h[:, 0:S], ALU.add, ALU.mult), y, a)
                        tmp.release(vs, y)
                        th[m] = (ts, h, y)
                    for m in group:
                        ts, h, y = th[m]
                        a = A(lambda e: e.activation(h[:, 0:S], h[:, 0:S], ACT.Sqrt), y)
                        y = V(lambda e: e.tensor_tensor(IG[:, m, :], IG[:, m, :], h[:, 0:S], ALU.mult), a)
                        tmp.release(ts, y)
                        rec[m] = V(lambda e: e.tensor_tensor_scan(IG[:, m, :], RG[:, m, :], IG[:, m, :], 0.0, ALU.mult, ALU.add), y)

                pipeline([recur(m) for m in range(10)])
                gd = []
                for m in range(10):
                    s1, p1, t1 = lru_in(m)
                    if m in (0, 1, 3, 5, 7):
                        g = (m + 1) // 2
                        scans([2 * g, 2 * g + 1])
                    ts, y0, tf = tmp.take()
                    a = A(lambda e: e.activation(y0[:, 0:S], p1[:, 0:S], ACT.Gelu_apprx_tanh), t1, tf)
                    pairs.release(s1, a)
                    y = V(lambda e: e.tensor_tensor(y0[:, 0:S], y0[:, 0:S], IG[:, m, :], ALU.mult), a, rec[m])
                    gd.append(split_into(Gh[:, m, :], Gl[:, m, :], y0[:, 0:S], y))
                    tmp.release(ts, gd[m])
                return add_out("lru_out", 10, lambda m: [(("lru_out", m, 640 * c, 640), list(range(5 * c, 5 * c + 5))) for c in range(2)], Gh, Gl, gd)

        with ExitStack() as ph:
            sqs, x_done = lru(sqs, x_done, ph)
        P.barrier()

        sqs, x_done = ffn(0, sqs, x_done)

        with ExitStack() as ph:
            gd = []
            inner = ExitStack()
            with inner:
                Q = sb("NQ", [128, 16, S], F32R, inner)
                KH = [sb(f"NKH{b}", [128, 4, S], F32R, inner) for b in range(2)]
                KL = [sb(f"NKL{b}", [128, 4, S], F32R, inner) for b in range(2)]
                VN = [sb(f"VN{b}", [128, 4, 4, 65], F32, inner) for b in range(2)]
                GT = sb("GT", [128, 4, 48], F32, inner)
                KCH = sb("KCH", [128, 128], F32R, inner)
                KCL = sb("KCL", [128, 128], F32R, inner)
                VB = sb("VB", [128, 4, 256], F32, inner)
                TB = sb("TB", [128, 512], F32, inner)
                RV = sb("RV", [128, 4], F32, inner)
                now = P.now()
                tb = [P.dma("sync", "tb", TB[:, :], t["ntab"][:, :], now), P.dma("sync", "rv", RV[:, :], t["rowok"][:, :], now)]
                von = [G(lambda e, b=b: e.memset(VN[b][:, :, :, 64:65], 1.0), now) for b in range(2)]
                vz = G(lambda e: e.memset(VB[:, :, :], 0.0), now)
                qd, kd, vd = [], [[], []], [[von[0]], [von[1]]]
                with ExitStack() as p2_:
                    Hh = sb("NHh", [128, 8, S], F32R, p2_)
                    Hl = sb("NHl", [128, 8, S], F32R, p2_)
                    hd = plain_rms("nsa_norm", sqs, Hh, Hl, x_done)

                    def nin(m):
                        return linear([(("nsa_in", m, 0, 1024), list(range(8)))], lambda k: (Hh[:, k, :], Hl[:, k, :]), R512, hd)

                    CF = sb("CF", [128, 4, 544], F32, p2_)
                    RH = sb("RH", [128, 8, 128], F32R, p2_)
                    RL = sb("RL", [128, 8, 128], F32R, p2_)
                    HID = sb("HID", [128, 2, 128], F32, p2_)
                    w2o = SM_AT["cmp_w2"][0]
                    cfz = G(lambda e: e.memset(CF[:, :, 504:544], 0.0), P.now())
                    cmpd, gtds = [], []

                    def others():
                        for m in range(8):
                            s1, p1, t1 = nin(m)
                            a = [stack_q(Q[:, 2 * m + f, :], p1[64 * f:64 * f + 64, 0:S], S, 0.125, t1) for f in range(2)]
                            pairs.release(s1, a)
                            qd.append(a)
                            yield
                        s1, p1, t1 = nin(20)
                        ts, gs, tf = tmp.take()
                        a = A(lambda e: e.activation(gs[:, 0:S], p1[:, 0:S], ACT.Sigmoid), t1, tf)
                        pairs.release(s1, a)
                        s2, p2, pf = pairs.take()
                        for i in range(4):
                            tok = MM(lambda e, i=i: e.transpose(p2[:, 128 * i:128 * i + 128], gs[:, 128 * i:128 * i + 128], ident), a, pf, inc=(i == 3))
                        tmp.release(ts, tok)
                        gtd = V(lambda e: e.tensor_copy(GT[:, :, :], p2[:, 0:512].rearrange("p (i n) -> p i n", i=4)[:, :, 0:48]), tok)
                        pairs.release(s2, gtd)
                        gtds.append(gtd)
                        yield
                        for b in range(2):
                            c0 = 8 + 4 * (b + 1)
                            for m in range(2):
                                s1, p1, t1 = nin(c0 + m)
                                ys = [stack_k(KH[b][:, 2 * m + f, :], KL[b][:, 2 * m + f, :], p1[64 * f:64 * f + 64, 0:S], S, t1) for f in range(2)]
                                pairs.release(s1, ys)
                                kd[b] += ys
                                yield
                            for m in range(2):
                                s1, p1, t1 = nin(c0 + 2 + m)
                                ts, vf, tf = tmp.take()
                                a = A(lambda e, vf=vf, p1=p1: e.activation(vf[:, 0:S], p1[:, 0:S], ACT.Copy), t1, tf)
                                pairs.release(s1, a)
                                s2, p2, pf = pairs.take()
                                for i in range(4):
                                    tok = MM(lambda e, i=i, vf=vf, p2=p2: e.transpose(p2[:, 128 * i:128 * i + 128], vf[:, 128 * i:128 * i + 128], ident), a, pf, inc=(i == 3))
                                tmp.release(ts, tok)
                                y = V(lambda e, m=m, b=b, p2=p2: e.tensor_copy(VN[b][:, :, 2 * m:2 * m + 2, 0:64], p2[:, 0:512].rearrange("p (i h d) -> p i h d", i=4, h=2)), tok)
                                pairs.release(s2, y)
                                vd[b].append(y)
                                yield

                    def compress():
                        prev = []
                        for kv in range(2):
                            cf = []
                            for m in range(2):
                                s1, p1, t1 = nin(8 + 2 * kv + m)
                                ys = []
                                for g in range(2):
                                    ys.append(V(lambda e, m=m, g=g, p1=p1: e.tensor_copy(CF[0:64, 2 * m + g, 0:S], p1[64 * g:64 * g + 64, 0:S]), t1, cfz, prev))
                                    ys.append(V(lambda e, m=m, g=g, p1=p1: e.tensor_copy(CF[64:128, 2 * m + g, 0:S - 1], p1[64 * g:64 * g + 64, 1:S]), t1, cfz, prev))
                                pairs.release(s1, ys)
                                cf += ys
                            po = SM_AT["cmp_pos"][0] + 16 * kv
                            acc = [pairs.take() for _ in range(2)]
                            for c in range(2):
                                rd = []
                                for k in range(8 * c, 8 * c + 8):
                                    ts, rr, tf = tmp.take()
                                    src = CF[:, :, 2 * k:2 * k + 512].rearrange("p g (j s) -> p g j s", s=16)[:, :, :, 0]
                                    y = V(lambda e: e.tensor_scalar(rr[:, 0:128].rearrange("p (g j) -> p g j", g=4), src, smc(po + k, po + k + 1), None, ALU.add), cf, tf)
                                    s = split_into(RH[:, k % 8, :], RL[:, k % 8, :], rr[:, 0:128], y, prev)
                                    tmp.release(ts, s)
                                    rd.append(s)
                                yield
                                for m in range(2):
                                    (hi, lo), ready, j = chunk("cmp_w1", 2 * kv + m, 1024 * c, 1024)
                                    for k in range(8):
                                        for q, (w, x) in enumerate(((hi, RH), (hi, RL), (lo, RH))):
                                            tok = MM(lambda e: e.matmul(acc[m][1][:, 0:128], w[:, 128 * k:128 * k + 128], x[:, k, :], start=(c == 0 and k == 0 and q == 0), stop=(c == 1 and k == 7 and q == 2)),
                                                     ready, rd[k], acc[m][2], inc=(k == 7 and q == 2))
                                    chunk_done(j, tok)
                                prev = [tok]
                            hd2 = []
                            for m in range(2):
                                s1, p1, _ = acc[m]
                                a = A(lambda e: e.activation(HID[:, m, :], p1[:, 0:128], ACT.Gelu_apprx_tanh, bias=sm("cmp_b1", 2 * kv + m, 1)), tok, prev, cmpd)
                                pairs.release(s1, a)
                                hd2.append(a)
                            yield
                            s1, p1, pf = pairs.take()
                            if kv == 0:
                                for hf in range(2):
                                    for k in range(2):
                                        tok = MM(lambda e, k=k, hf=hf, p1=p1: e.matmul(p1[64 * hf:64 * hf + 64, 0:128], smc(w2o + 64 * k, w2o + 64 * k + 64), HID[:, k, :], start=(k == 0), stop=(k == 1)), hd2, pf)
                                y = A(lambda e: e.activation(KCH[:, :], p1[:, 0:128], ACT.Copy), tok)
                                y = V(lambda e: e.scalar_tensor_tensor(KCL[:, :], p1[:, 0:128], 1.0, KCH[:, :].bitcast(F32), ALU.mult, ALU.subtract), y)
                                cmpd.append(y)
                                prev = [y]
                            else:
                                for g in range(4):
                                    for k in range(2):
                                        hsrc = HID[:, k, 32 * g:32 * g + 32]
                                        for q in range(4):
                                            tok = MM(lambda e, k=k, g=g, q=q, hsrc=hsrc, p1=p1: e.matmul(p1[32 * q:32 * q + 32, 64 * g:64 * g + 64], hsrc, smc(w2o + 128 + 64 * k, w2o + 192 + 64 * k), start=(k == 0), stop=(k == 1), skip_group_check=True), hd2, pf)
                                y = []
                                for q in range(4):
                                    y.append(V(lambda e, q=q, p1=p1: e.tensor_copy(VB[32 * q:32 * q + 32, :, 64 * q:64 * q + 64], p1[32 * q:32 * q + 32, 0:256].rearrange("p (g d) -> p g d", g=4)), tok, vz))
                                cmpd.extend(y)
                            pairs.release(s1, y)

                    ga, gb = compress(), others()
                    while next(ga, "end") != "end":
                        for _ in range(3):
                            next(gb, None)
                    for _ in gb:
                        pass
                    gtd = gtds[0]
                P.barrier()
                OT = [sb(f"OT{i}", [128, 1024], F32, inner) for i in range(4)]
                CB = [sb(f"CB{i}", [128, 512], F32, inner) for i in range(2)]
                PR = [sb(f"PR{i}", [128, 1024], F32, inner) for i in range(3)]
                PT = [sb(f"PT{i}", [128, 1024], F32, inner) for i in range(2)]
                prob, prot = Ring(PR), Ring(PT)
                cbr = Ring(CB)

                def halves(ap, n):
                    return ap.rearrange("p (b c) -> p b c", b=2)[:, :, 0:n]

                def nsa_attention(steps):
                    sring, lent = pairs.lend([0, 1, 2]), pairs.lend([3])
                    oring = Ring([lent.items[0][:, 512 * i:512 * i + 512] for i in range(2)])
                    oring.free = [lent.free[0] for _ in oring.items]

                    def first(s):
                        qt, nw, nh, h0 = s["qt"], s["nw"], s["nh"], s["h"]
                        w = nw * nh
                        slot, ps, free = sring.take()
                        for b in range(2):
                            for j in range(nh):
                                c = 512 * b + nw * j
                                q, g = Q[:, h0 + j, 128 * qt:128 * qt + 128], (h0 + j) // 4
                                MM(lambda e: e.matmul(ps[:, c:c + nw], q, KH[b][:, g, 0:nw], start=True, stop=False), free, qd, kd[b], inc=False)
                                tok = MM(lambda e: e.matmul(ps[:, c:c + nw], q, KL[b][:, g, 0:nw], start=False, stop=True), inc=(j == nh - 1))
                        for j in range(nh):
                            pj = ps.rearrange("p (b c) -> p b c", b=2)[:, :, nw * j:nw * j + nw]
                            tj = TB[:, 512 - nw:512].unsqueeze(1).broadcast_to([128, 2, nw])
                            y = V(lambda e: e.scalar_tensor_tensor(pj, tj, -slopes[h0 + j], pj, ALU.mult, ALU.add), tok, tb)
                        s.update(sps=ps, sslot=slot, y=y)

                    def peak(s):
                        nw, nh, ps, y = s["nw"], s["nh"], s["sps"], s["y"]
                        ss, sv, sf = stat.take()
                        m = V(lambda e: e.tensor_reduce(sv[:, 0:2 * nh].rearrange("p (b j) -> p b j", b=2),
                                                        halves(ps, nh * nw).rearrange("p b (j c) -> p b j c", j=nh), AX.X, ALU.max, negate=True), y, sf)
                        s.update(ss=ss, sv=sv, m=m)

                    def expo(s):
                        nw, nh, ps, sv, m = s["nw"], s["nh"], s["sps"], s["sv"], s["m"]
                        pslot, pr, pf = prob.take()
                        for b in range(2):
                            for j in range(nh):
                                c, i = 512 * b + nw * j, b * nh + j
                                x = A(lambda e: e.activation(pr[:, c:c + nw], ps[:, c:c + nw], ACT.Exp, bias=sv[:, i:i + 1]), m, pf)
                        s.update(pslot=pslot, pr=pr, x=x)

                    def second(s):
                        w, pr = s["nw"] * s["nh"], s["pr"]
                        ps = s["sps"]
                        for b in range(2):
                            for i in range(w // 128):
                                c = 512 * b + 128 * i
                                tok = MM(lambda e: e.transpose(ps[:, c:c + 128], pr[:, c:c + 128], ident), s["x"], inc=(i == w // 128 - 1))
                        prob.release(s["pslot"], tok)
                        qslot, pt, qf = prot.take()
                        y = [A(lambda e: e.activation(pt[:, 0:w], ps[:, 0:w], ACT.Copy), tok, qf)]
                        if s["nh"] == 1:
                            y.append(A(lambda e: e.activation(pt[:, 512:512 + w], ps[:, 512:512 + w], ACT.Copy), tok, qf))
                        else:
                            y.append(V(lambda e: e.tensor_copy(pt[:, 512:512 + w], ps[:, 512:512 + w]), tok, qf))
                        sring.release(s["sslot"], y)
                        s.update(qslot=qslot, pt=pt, y=y)

                    def third(s):
                        qt, nw, nh, h0, ot, last = s["qt"], s["nw"], s["nh"], s["h"], s["ot"], s["last"]
                        pt, ss, sv = s["pt"], s["ss"], s["sv"]
                        s["tslot"], ps, free = oring.take()
                        s["tps"] = ps
                        ob = 65 * nh
                        nb = nw // 128
                        for b in range(2):
                            for j in range(nh):
                                o, g = ob * b + 65 * j, (h0 + j) // 4
                                for i in range(nb):
                                    c = 512 * b + nw * j + 128 * i
                                    tok = MM(lambda e: e.matmul(ps[:, o:o + 65], pt[:, c:c + 128], VN[b][:, i, g, :], start=(i == 0), stop=(i == nb - 1)),
                                             free, s["y"] if b else s["y"][0], vd[b], inc=(i == nb - 1))
                        prot.release(s["qslot"], tok)
                        o4 = ps[:, 0:130 * nh].rearrange("p (b j d) -> p b j d", b=2, j=nh)
                        r3 = sv[:, 0:2 * nh].rearrange("p (b j) -> p b j", b=2)
                        g3 = GT[:, qt, 16:48].rearrange("p (b h) -> p b h", b=2)[:, :, h0:h0 + nh]
                        d = V(lambda e: e.reciprocal(r3, o4[:, :, :, 64]), tok, s["x"])
                        s.update(d=d, r3=r3, g3=g3)

                    def gate(s):
                        s["d"] = V(lambda e: e.tensor_tensor(s["r3"], s["r3"], s["g3"], ALU.mult), s["d"], gtd)

                    def finish(s):
                        nh, h0, ot, last, ps, ss, sv, d = (s[k] for k in ("nh", "h", "ot", "last", "tps", "ss", "sv", "d"))
                        y = last["t"]
                        done = []
                        for b in range(2):
                            for j in range(nh):
                                o, i, c = 65 * (nh * b + j), nh * b + j, 64 * (h0 + j)
                                y = V(lambda e: e.scalar_tensor_tensor(ot[:, c:c + 64], ps[:, o:o + 64], sv[:, i:i + 1], ot[:, c:c + 64], ALU.mult, ALU.add), d, done[j] if b else last["t"])
                                done.append(y)
                        oring.release(s["tslot"], y)
                        d = y
                        stat.release(ss, d)
                        last["t"] = y

                    n = len(steps)
                    for i in range(n + 4):
                        if i < n:
                            first(steps[i])
                        if i >= 4:
                            finish(steps[i - 4])
                        if i < n:
                            peak(steps[i])
                        if 2 <= i < n + 2:
                            second(steps[i - 2])
                        if 3 <= i < n + 3:
                            third(steps[i - 3])
                        if i < n:
                            expo(steps[i])
                        if 3 <= i < n + 3:
                            gate(steps[i - 3])
                    lent.free[0] = list(oring.free)
                    pairs.give_back(sring, [0, 1, 2])
                    pairs.give_back(lent, [3])

                slopes = [float(np.float32(2.0 ** (-8.0 * (h + 1) / 16))) for h in range(16)]
                last = [None] * 4

                def compressed(qt):
                    ot = OT[qt]
                    cslot, cb, cf = cbr.take()
                    d = P.dma("sync", f"cb{cslot}", cb[:, :], t["ctab"][qt, :, :], cf)
                    s1, p1, pf = pairs.take()
                    for h in range(16):
                        g = h // 4
                        MM(lambda e: e.matmul(p1[:, 32 * h:32 * h + 32], Q[:, h, 128 * qt:128 * qt + 128], KCH[:, 32 * g:32 * g + 32], start=True, stop=False), qd, cmpd, pf, inc=False)
                        tok = MM(lambda e: e.matmul(p1[:, 32 * h:32 * h + 32], Q[:, h, 128 * qt:128 * qt + 128], KCL[:, 32 * g:32 * g + 32], start=False, stop=True), inc=(h == 15))
                    ts, pc, tf = prob.take()
                    ss, sv, sf = tmp.take()
                    y = V(lambda e: e.tensor_tensor(pc[:, 0:512], p1[:, 0:512], cb[:, :], ALU.add), tok, d, tf, now)
                    cbr.release(cslot, y)
                    pairs.release(s1, y)
                    pc3 = pc[:, 0:512].rearrange("p (h j) -> p h j", h=16)
                    y = V(lambda e: e.tensor_reduce(sv[:, 0:16], pc3, AX.X, ALU.max), y, sf)
                    y = V(lambda e: e.tensor_tensor(pc3, pc3, sv[:, 0:16].unsqueeze(2).broadcast_to([128, 16, 32]), ALU.subtract), y)
                    a = A(lambda e: e.activation(pc[:, 0:512], pc[:, 0:512], ACT.Exp), y)
                    yield
                    s2, p2, pf = pairs.take()
                    for i in range(4):
                        tok = MM(lambda e: e.transpose(p2[:, 128 * i:128 * i + 128], pc[:, 128 * i:128 * i + 128], ident), a, pf, inc=(i == 3))
                    us, pt, uf = prot.take()
                    b = A(lambda e: e.activation(pt[:, 0:512], p2[:, 0:512], ACT.Copy), tok, uf)
                    pairs.release(s2, b)
                    y = V(lambda e: e.tensor_reduce(sv[:, 16:32], pc3, AX.X, ALU.add), a)
                    prob.release(ts, y, b)
                    y = V(lambda e: e.reciprocal(sv[:, 32:48], sv[:, 16:32]), y)
                    y = V(lambda e: e.scalar_tensor_tensor(sv[:, 48:64], sv[:, 32:48], RV[:, qt:qt + 1], GT[:, qt, 0:16], ALU.mult, ALU.mult), y, gtd, tb)
                    yield
                    s3, p3, pf = pairs.take()
                    for g in range(4):
                        tok = MM(lambda e: e.matmul(p3[:, 256 * g:256 * g + 256], pt[:, 128 * g:128 * g + 128], VB[:, g, :], start=True, stop=True), b, pf, cmpd, inc=(g == 3))
                    prot.release(us, tok)
                    od = V(lambda e: e.tensor_tensor(ot[:, :].rearrange("p (h d) -> p h d", h=16), p3.rearrange("p (h d) -> p h d", h=16), sv[:, 48:64].unsqueeze(2).broadcast_to([128, 16, 64]), ALU.mult), tok, y)
                    pairs.release(s3, od)
                    tmp.release(ss, od)
                    last[qt] = {"t": od}

                pipeline([compressed(qt) for qt in range(4)])
                nsa_attention([dict(qt=qt, nw=128 * qt + 128, nh=nh, h=h, ot=OT[qt], last=last[qt])
                               for qt, nh in ((0, 2), (1, 2), (2, 1), (3, 1)) for h in range(0, 16, nh)])
                qread = P.now()
                Gh, Gl = Q[:, 0:8, :], Q[:, 8:16, :]
                for qt in range(4):
                    s1, p1, pf = pairs.take()
                    for i in range(8):
                        tok = MM(lambda e: e.transpose(p1[:, 128 * i:128 * i + 128], OT[qt][:, 128 * i:128 * i + 128], ident), last[qt]["t"], pf, inc=(i == 7))
                    p8 = p1.rearrange("p (m n) -> p m n", m=8)
                    s = split_into(Gh[:, :, 128 * qt:128 * qt + 128], Gl[:, :, 128 * qt:128 * qt + 128], p8, tok, qread)
                    pairs.release(s1, s)
                    gd.append(s)
                sqs, x_done = add_out("nsa_out", 8, lambda m: [(("nsa_out", m, 0, 1024), list(range(8)))], Gh, Gl, [gd] * 8)
        P.barrier()

        sqs, x_done = ffn(1, sqs, x_done)

        rs, ri, r = sqs.root()
        fd = [V(lambda e, k=k: e.scalar_tensor_tensor(X[:, k, 0:S], X[:, k, 0:S], sm("final_g", k, 1), ri[:, 0:S], ALU.mult, ALU.mult), r, x_done) for k in range(8)]
        with ExitStack() as ph:
            OU = [sb(f"OU{i}", [128, 1024], F32, ph) for i in range(2)]
            our = Ring(OU)
            outs = []
            for i in range(4):
                slot, ps, free = pairs.take()
                for k in range(8):
                    tok = MM(lambda e, i=i, k=k, ps=ps: e.transpose(ps[:, 128 * k:128 * k + 128], X[:, k, 128 * i:128 * i + 128], ident), fd, free, inc=(k == 7))
                os_, ou, of = our.take()
                y = V(lambda e, ou=ou, ps=ps: e.tensor_copy(ou[:, 0:512], ps[:, 0:512]), tok, of)
                z = A(lambda e, ou=ou, ps=ps: e.activation(ou[:, 512:1024], ps[:, 512:1024], ACT.Copy), tok, of)
                pairs.release(slot, y, z)
                d = P.dma("sync", f"ou{os_}", out[128 * i:128 * i + 128, :], ou[:, :], y, z)
                our.release(os_, d)
                outs.append(d)
        P.queue["sync"].append((flat(outs), None, None, 0))
        if order:
            P.emit(nc, sems)
    return log


DMA_SEMS = [f"w{i}" for i in range(NRAW)] + [f"mw{i}" for i in range(NMOD)] + ["sm", "sm2", "co", "xt0", "xt1", "xt2", "xt3", "xt4", "xt5",  "rc", "mk", "bi0", "bi1",  "tb", "rv", "cb0", "cb1", "ou0", "ou1"]


def program(nc, make, t, out):
    order = build(make(), t, out, [], {})
    with ExitStack() as ctx:
        sems = {name: ctx.enter_context(nc.semaphore("s_" + name)) for name in list(ENGINES) + DMA_SEMS}
        build(nc, t, out, order, sems)


def constants():
    co = np.zeros((128, 512), np.float32)
    co[:, 0:128] = np.eye(128)
    co[:, 128:256] = 1
    co[0:64, 256:320] = 1
    co[64:128, 320:384] = 1
    for m in range(128):
        if m % 32 < 16:
            co[m + 16, 384 + m] = -1
        else:
            co[m - 16, 384 + m] = 1
    inv = np.float32(10000.0) ** (-np.arange(16, dtype=np.float32) / np.float32(16))
    s = np.arange(S)
    rope = np.zeros((128, 1024), np.float32)
    for p in range(128):
        pos = (s // 64 if (p % 64) < 32 else s % 64).astype(np.float32)
        ang = pos * inv[p % 16]
        rope[p, 0:S] = np.cos(ang)
        rope[p, S:] = np.sin(ang)
    p = np.arange(128)[:, None]
    y = np.arange(384)[None, :]
    wmask = np.where(np.abs(y - 128 - p) <= 128, 0.0, NEG).astype(np.float32)
    y = np.arange(512)[None, :] - 384
    ntab = np.where(p >= y, p - y, FAR).astype(np.float32)
    sl = 2.0 ** (-8.0 * np.arange(1, 17) / 16)
    ctab = np.zeros((4, 128, 16, 32), np.float32)
    rowok = np.zeros((128, 4), np.float32)
    for qt in range(4):
        tt = 128 * qt + np.arange(128)
        j = np.arange(32)
        dist = tt[:, None] - (16 * j[None, :] + 15.5)
        ok = (16 * j[None, :] + 31 <= tt[:, None]) & (j[None, :] < 31)
        ctab[qt] = np.where(ok[:, None, :], -sl.astype(np.float32)[None, :, None] * dist.astype(np.float32)[:, None, :], NEG)
        rowok[:, qt] = ok.any(1)
    return {"co": co, "rope": rope, "wmask": wmask, "ntab": ntab, "ctab": ctab.reshape(4, 128, 512), "rowok": rowok}


def pack(w):
    k, n = w.shape
    if n % 128:
        w = np.concatenate([w, np.zeros((k, 128 - n % 128), w.dtype)], 1)
        n = w.shape[1]
    return np.ascontiguousarray(w.reshape(k // 128, 128, n // 128, 128).transpose(2, 1, 0, 3).reshape(n // 128, 128, k))


def layout(i):
    d = dict(constants())
    d["x"], d["ctx"] = i["x"][0], i["ctx"][0]
    for l in range(2):
        d[f"w_ada{l}"] = i["w_ada"][l].reshape(8, 128, 4, 768).transpose(2, 0, 1, 3).reshape(32, 128, 768)
        for n in ("w_in", "w_proj_a", "w_proj_b", "w_proj_c", "w_o"):
            d[f"{n}{l}"] = pack(i[n][l])
        pad = np.full((8, 15, 64, 64), NEG, np.float32)
        for j in range(64):
            c0 = min(max(j - 8, 0), 48)
            pad[:, :, j, c0:c0 + 16] = i["na_rpb"][l][:, :, c0 - j + 15:c0 - j + 31]
        b = np.zeros((8, 2, 64, 15, 64), np.float32)
        tab = pad.transpose(0, 2, 1, 3)
        b[:, 0] = tab
        b[:, 1, :, 1:] = tab[:, :, :14]
        d[f"rpb{l}"] = b.reshape(8, 128, 960)
        d[f"ffn_in{l}"] = pack(i["ffn_w_in_2"][l])
        d[f"ffn_out{l}"] = pack(i["ffn_w_out_2"][l])
    d["lru_in"] = pack(i["lru_w_in_2"][0])
    d["lru_out"] = pack(i["lru_w_out_2"][0])
    d["gate_w"] = i["lru_gate_w_2"][0].transpose(1, 2, 0, 3).reshape(10, 128, 256)
    d["nsa_in"] = pack(i["nsa_w_in_2"][0])
    d["nsa_out"] = pack(i["nsa_w_out_2"][0])
    d["cmp_w1"] = np.concatenate([pack(i["nsa_cmp_w1_2"][0, k]) for k in range(2)])
    sm = np.zeros((128, SM_N), np.float32)

    def put(name, a):
        o, w = SM_AT[name]
        sm[:, o:o + w] = a.reshape(a.shape[0], -1)

    def col(v):
        return v.reshape(-1, 128).T

    put("cc", np.stack([col(i["c"][0]), col(i["c_ctx"])], 2))
    for l in range(2):
        put(f"norm_g{l}", col(i["norm_g"][l]))
        put(f"b_ada{l}", col(i["b_ada"][l]))
        put(f"conv_w{l}", i["conv_w"][l].reshape(31, 4, 128).transpose(2, 1, 0))
        put(f"conv_b{l}", col(i["conv_b"][l]))
        put(f"cln_g{l}", col(i["cln_g"][l]))
        put(f"cln_b{l}", col(i["cln_b"][l]))
        for a, b in (("na_q", "na_q_norm"), ("na_k", "na_k_norm"), ("wa_q", "wa_q_norm"), ("wa_k", "wa_k_norm")):
            put(f"{a}{l}", np.tile(i[b][l], 2)[:, None])
        put(f"sink{l}", np.tile(i["wa_sink"][l][None], (128, 1)))
        put(f"ffn_norm{l}", col(i["ffn_norm_g_2"][l]))
        put(f"ffn_cw{l}", i["ffn_conv_w_2"][l].reshape(3, 24, 128).transpose(2, 1, 0))
        put(f"ffn_cb{l}", col(i["ffn_conv_b_2"][l]))
    put("lru_norm", col(i["lru_norm_g_2"][0]))
    put("lru_conv_w", i["lru_conv_w_2"][0].reshape(4, 10, 128).transpose(2, 1, 0))
    put("lru_conv_b", col(i["lru_conv_b_2"][0]))
    put("gate_b", i["lru_gate_b_2"][0].reshape(2, 10, 128).transpose(2, 0, 1))
    put("a_param", col(i["lru_a_param_2"][0]))
    put("nsa_norm", col(i["nsa_norm_g_2"][0]))
    put("cmp_pos", i["nsa_cmp_pos_2"][0].reshape(2, 16, 128).transpose(2, 0, 1))
    put("cmp_b1", i["nsa_cmp_b1_2"][0].reshape(2, 2, 128).transpose(2, 0, 1))
    put("cmp_w2", i["nsa_cmp_w2_2"][0].reshape(2, 2, 128, 64).transpose(2, 0, 1, 3))
    put("final_g", col(i["final_norm_g_2"]))
    d["sm"] = sm
    return d


def kernel(**inputs):
    import concourse.bacc as bacc
    from concourse.bass_utils import run_bass_kernel_spmd

    i = {k: np.asarray(v) for k, v in inputs.items()}
    d = layout(i)

    def make():
        return bacc.Bacc("TRN2", target_bir_lowering=False, num_devices=1)

    nc = make()
    arrays, t = {}, {}
    for name, a in d.items():
        a = np.ascontiguousarray(a, dtype=np.float32)
        arrays[f"in_{name}"] = a
        t[name] = nc.dram_tensor(f"in_{name}", a.shape, F32, kind="ExternalInput").ap()
    out = nc.dram_tensor("out_0", (S, 1024), F32, kind="ExternalOutput").ap()
    program(nc, make, t, out)
    r = run_bass_kernel_spmd(nc, [arrays], core_ids=[0])
    return r.results[0]["out_0"].reshape(1, S, 1024)
```
